# Optimizing a Trainium2 kernel written in Bass

```python
import jax, jax.numpy as jnp
from jax import lax
import numpy as np

D_MODEL = 2048
BATCH = 1
SEQ = 256
DEPTH = 1

HEAD_DIM = 128
N_HEADS_DSA = 8
N_HEADS_MOBA = 8
KV_LATENT = 256
IDX_HEADS = 16
IDX_DIM = 64
DSA_TOPK_MAX = 256
MOBA_BLOCK = 256
MOBA_TOPK_MAX = 3
N_MEM = 256
N_HEADS_MEM = 4
D_FF = -(-8 * D_MODEL // (3 * 256)) * 256
ATTN_Q_BLOCK = 128
MOBA_Q_BLOCK = 64
DSA_WIDTH = N_HEADS_DSA * HEAD_DIM
MOBA_WIDTH = N_HEADS_MOBA * HEAD_DIM
MEM_WIDTH = N_HEADS_MEM * HEAD_DIM
SPLIT_SIZES = (DSA_WIDTH, KV_LATENT, IDX_HEADS * IDX_DIM, IDX_DIM, IDX_HEADS,
               MOBA_WIDTH, MOBA_WIDTH, MOBA_WIDTH, D_MODEL, D_MODEL)
IN_WIDTH = sum(SPLIT_SIZES)
ALPHA = (2.0 * DEPTH) ** 0.25
BETA = (8.0 * DEPTH) ** -0.25
LN_EPS = 1e-5


def layer_norm(x, g, b):
    xf = x.astype(jnp.float32)
    mu = xf.mean(-1, keepdims=True)
    var = jnp.square(xf - mu).mean(-1, keepdims=True)
    return ((xf - mu) * lax.rsqrt(var + LN_EPS) * g.astype(jnp.float32) + b.astype(jnp.float32)).astype(x.dtype)

def rms_norm(x, g):
    xf = x.astype(jnp.float32)
    return (xf * lax.rsqrt(jnp.mean(xf * xf, -1, keepdims=True) + LN_EPS) * g.astype(jnp.float32)).astype(x.dtype)

def alibi_slopes(n):
    return jnp.asarray([2.0 ** (-8.0 * (i + 1) / n) for i in range(n)], dtype=jnp.float32)

def dsa_attention(q, c_kv, q_idx, k_idx, w_idx, w_uk, w_uv):
    S = q.shape[0]
    topk = min(DSA_TOPK_MAX, S // 4)
    slopes = alibi_slopes(N_HEADS_DSA)
    q_lat = jnp.einsum('shd,hdc->shc', q, w_uk)
    key_pos = jnp.arange(S)
    idx_scale = IDX_DIM ** -0.5
    w_scale = IDX_HEADS ** -0.5

    def block(i):
        t0 = i * ATTN_Q_BLOCK
        qi = lax.dynamic_slice_in_dim(q_idx, t0, ATTN_Q_BLOCK, 0)
        wi = lax.dynamic_slice_in_dim(w_idx, t0, ATTN_Q_BLOCK, 0)
        ql = lax.dynamic_slice_in_dim(q_lat, t0, ATTN_Q_BLOCK, 0)
        qpos = t0 + jnp.arange(ATTN_Q_BLOCK)
        logits = jnp.einsum('thd,sd->ths', qi, k_idx, preferred_element_type=jnp.float32) * idx_scale
        score = jnp.einsum('th,ths->ts', wi.astype(jnp.float32) * w_scale, jax.nn.relu(logits))
        score = jnp.where(key_pos[None, :] <= qpos[:, None], score, -jnp.inf)
        _, sel = lax.top_k(score, topk)
        valid = sel <= qpos[:, None]
        c_sel = c_kv[sel]
        s = jnp.einsum('thc,tkc->thk', ql, c_sel, preferred_element_type=jnp.float32) * (HEAD_DIM ** -0.5)
        dist = (qpos[:, None] - sel).astype(jnp.float32)
        s = s - slopes[None, :, None] * dist[:, None, :]
        s = jnp.where(valid[:, None, :], s, -jnp.inf)
        p = jax.nn.softmax(s, axis=-1).astype(c_kv.dtype)
        return jnp.einsum('thk,tkc->thc', p, c_sel)

    o_lat = lax.map(block, jnp.arange(S // ATTN_Q_BLOCK)).reshape(S, N_HEADS_DSA, KV_LATENT)
    o = jnp.einsum('shc,hcd->shd', o_lat, w_uv)
    return o.reshape(S, DSA_WIDTH)

def moba_attention(q, k, v):
    S, H, Dh = q.shape
    n_blk = -(-S // MOBA_BLOCK)
    pad = n_blk * MOBA_BLOCK - S
    kb = jnp.pad(k, ((0, pad), (0, 0), (0, 0))).reshape(n_blk, MOBA_BLOCK, H, Dh).transpose(2, 0, 1, 3)
    vb = jnp.pad(v, ((0, pad), (0, 0), (0, 0))).reshape(n_blk, MOBA_BLOCK, H, Dh).transpose(2, 0, 1, 3)
    k_mean = kb.astype(jnp.float32).mean(axis=2)
    n_sel = min(MOBA_TOPK_MAX, n_blk - 1)
    n_past = n_sel * MOBA_BLOCK
    slopes = alibi_slopes(H)
    scale = Dh ** -0.5
    offs = jnp.arange(MOBA_BLOCK)
    blk_ids = jnp.arange(n_blk)
    head_ix = jnp.arange(H)[None, :, None]

    def block(i):
        t0 = i * MOBA_Q_BLOCK
        qi = lax.dynamic_slice_in_dim(q, t0, MOBA_Q_BLOCK, 0)
        qpos = t0 + jnp.arange(MOBA_Q_BLOCK)
        own = t0 // MOBA_BLOCK
        k_own = lax.dynamic_index_in_dim(kb, own, axis=1, keepdims=False)
        v_own = lax.dynamic_index_in_dim(vb, own, axis=1, keepdims=False)
        own_pos = own * MOBA_BLOCK + offs
        s_own = jnp.einsum('thd,hkd->thk', qi, k_own, preferred_element_type=jnp.float32) * scale
        s_own = s_own - slopes[None, :, None] * (qpos[:, None] - own_pos[None, :]).astype(jnp.float32)[:, None, :]
        s_own = jnp.where((own_pos[None, :] <= qpos[:, None])[:, None, :], s_own, -jnp.inf)
        if n_sel == 0:
            p = jax.nn.softmax(s_own, axis=-1).astype(v.dtype)
            return jnp.einsum('thk,hkd->thd', p, v_own)
        gate = jnp.einsum('thd,hnd->thn', qi.astype(jnp.float32), k_mean)
        gate = jnp.where(blk_ids[None, None, :] < own, gate, -jnp.inf)
        _, sel = lax.top_k(gate, n_sel)
        k_sel = kb[head_ix, sel]
        v_sel = vb[head_ix, sel].reshape(MOBA_Q_BLOCK, H, n_past, Dh)
        pos_sel = sel[..., None] * MOBA_BLOCK + offs
        s_sel = jnp.einsum('thd,thnkd->thnk', qi, k_sel, preferred_element_type=jnp.float32) * scale
        s_sel = s_sel - slopes[None, :, None, None] * (qpos[:, None, None, None] - pos_sel).astype(jnp.float32)
        s_sel = jnp.where((sel < own)[..., None], s_sel, -jnp.inf).reshape(MOBA_Q_BLOCK, H, n_past)
        s = jnp.concatenate([s_sel, s_own], axis=-1)
        p = jax.nn.softmax(s, axis=-1).astype(v.dtype)
        return (jnp.einsum('thk,thkd->thd', p[..., :n_past], v_sel)
                + jnp.einsum('thk,hkd->thd', p[..., n_past:], v_own))

    o = lax.map(block, jnp.arange(S // MOBA_Q_BLOCK))
    return o.reshape(S, H * Dh)

def hybrid_mixer(x, w_in, b_gate, kv_norm_g, idx_k_norm_g, idx_k_norm_b, w_uk, w_uv, w_o_dsa, w_o_moba, w_out):
    B, S, _ = x.shape
    points = np.cumsum(SPLIT_SIZES)[:-1].tolist()
    proj = x @ w_in
    q_dsa, c_kv, q_idx, k_idx, w_idx, q_m, k_m, v_m, ga, gb = jnp.split(proj, points, axis=-1)
    c_kv = rms_norm(c_kv, kv_norm_g)
    k_idx = layer_norm(k_idx, idx_k_norm_g, idx_k_norm_b)
    q_dsa = q_dsa.reshape(B, S, N_HEADS_DSA, HEAD_DIM)
    q_idx = q_idx.reshape(B, S, IDX_HEADS, IDX_DIM)
    o_a = jax.vmap(dsa_attention, in_axes=(0, 0, 0, 0, 0, None, None))(q_dsa, c_kv, q_idx, k_idx, w_idx, w_uk, w_uv)
    hm = (B, S, N_HEADS_MOBA, HEAD_DIM)
    o_b = jax.vmap(moba_attention)(q_m.reshape(hm), k_m.reshape(hm), v_m.reshape(hm))
    g_a = jax.nn.sigmoid(ga + b_gate[0])
    g_b = jax.nn.sigmoid(gb + b_gate[1])
    merged = g_a * (o_a @ w_o_dsa) + g_b * (o_b @ w_o_moba)
    return merged @ w_out

def mem_cross_attention(x, mem, w_q, w_kv, w_o):
    B, S, _ = x.shape
    q = (x @ w_q).reshape(B, S, N_HEADS_MEM, HEAD_DIM)
    k, v = jnp.split(mem @ w_kv, 2, axis=-1)
    k = k.reshape(B, N_MEM, N_HEADS_MEM, HEAD_DIM)
    v = v.reshape(B, N_MEM, N_HEADS_MEM, HEAD_DIM)
    s = jnp.einsum('bshd,bmhd->bhsm', q, k, preferred_element_type=jnp.float32) * (HEAD_DIM ** -0.5)
    p = jax.nn.softmax(s, axis=-1).astype(x.dtype)
    o = jnp.einsum('bhsm,bmhd->bshd', p, v).reshape(B, S, MEM_WIDTH)
    return o @ w_o

def swiglu(x, w_in, w_out):
    g, u = jnp.split(x @ w_in, 2, axis=-1)
    return (jax.nn.silu(g) * u) @ w_out

def first_inputs(seed: int = 0) -> dict:
    key = jax.random.key(seed)
    ks = jax.random.split(key, 20)
    f32 = jnp.float32

    def nrm(k, shape, scale):
        return jax.random.normal(k, shape, f32) * scale

    v_off = sum(SPLIT_SIZES[:7])
    col_scale = jnp.ones((IN_WIDTH,), f32).at[v_off:v_off + MOBA_WIDTH].set(BETA)
    kv_scale = jnp.ones((2 * MEM_WIDTH,), f32).at[MEM_WIDTH:].set(BETA)
    return {
        'x': nrm(ks[0], (BATCH, SEQ, D_MODEL), 1.0),
        'mem': nrm(ks[1], (BATCH, N_MEM, D_MODEL), 1.0),
        'w_in': nrm(ks[2], (DEPTH, D_MODEL, IN_WIDTH), D_MODEL ** -0.5) * col_scale,
        'b_gate': nrm(ks[3], (DEPTH, 2, D_MODEL), 0.02),
        'kv_norm_g': 1.0 + nrm(ks[4], (DEPTH, KV_LATENT), 0.02),
        'idx_k_norm_g': 1.0 + nrm(ks[5], (DEPTH, IDX_DIM), 0.02),
        'idx_k_norm_b': nrm(ks[6], (DEPTH, IDX_DIM), 0.02),
        'w_uk': nrm(ks[7], (DEPTH, N_HEADS_DSA, HEAD_DIM, KV_LATENT), HEAD_DIM ** -0.5),
        'w_uv': nrm(ks[8], (DEPTH, N_HEADS_DSA, KV_LATENT, HEAD_DIM), BETA * KV_LATENT ** -0.5),
        'w_o_dsa': nrm(ks[9], (DEPTH, DSA_WIDTH, D_MODEL), BETA * DSA_WIDTH ** -0.5),
        'w_o_moba': nrm(ks[10], (DEPTH, MOBA_WIDTH, D_MODEL), BETA * MOBA_WIDTH ** -0.5),
        'w_out': nrm(ks[11], (DEPTH, D_MODEL, D_MODEL), BETA * D_MODEL ** -0.5),
        'w_q_mem': nrm(ks[12], (DEPTH, D_MODEL, MEM_WIDTH), D_MODEL ** -0.5),
        'w_kv_mem': nrm(ks[13], (DEPTH, D_MODEL, 2 * MEM_WIDTH), D_MODEL ** -0.5) * kv_scale,
        'w_o_mem': nrm(ks[14], (DEPTH, MEM_WIDTH, D_MODEL), BETA * MEM_WIDTH ** -0.5),
        'w_ffn_in': nrm(ks[15], (DEPTH, D_MODEL, 2 * D_FF), BETA * D_MODEL ** -0.5),
        'w_ffn_out': nrm(ks[16], (DEPTH, D_FF, D_MODEL), BETA * D_FF ** -0.5),
        'ln_g': 1.0 + nrm(ks[17], (DEPTH, 3, D_MODEL), 0.02),
        'ln_b': nrm(ks[18], (DEPTH, 3, D_MODEL), 0.02),
    }

def first_block(x, mem, w_in, b_gate, kv_norm_g, idx_k_norm_g, idx_k_norm_b, w_uk, w_uv, w_o_dsa, w_o_moba,
              w_out, w_q_mem, w_kv_mem, w_o_mem, w_ffn_in, w_ffn_out, ln_g, ln_b):
    for l in range(DEPTH):
        y = hybrid_mixer(x, w_in[l], b_gate[l], kv_norm_g[l], idx_k_norm_g[l], idx_k_norm_b[l], w_uk[l], w_uv[l],
                         w_o_dsa[l], w_o_moba[l], w_out[l])
        x = layer_norm(ALPHA * x + y, ln_g[l, 0], ln_b[l, 0])
        y = mem_cross_attention(x, mem, w_q_mem[l], w_kv_mem[l], w_o_mem[l])
        x = layer_norm(ALPHA * x + y, ln_g[l, 1], ln_b[l, 1])
        y = swiglu(x, w_ffn_in[l], w_ffn_out[l])
        x = layer_norm(ALPHA * x + y, ln_g[l, 2], ln_b[l, 2])
    return x


CHUNK = 64
Q_BLOCK = 128
N_HEADS = 4
BRANCH_W = N_HEADS * HEAD_DIM
N_BRANCH = 3
LEFT_CHUNKS = 8
BAND = (LEFT_CHUNKS + 1) * CHUNK
MAX_REL = 128
N_REL = 2 * MAX_REL + 1
QKVG_COLS = N_BRANCH * 4 * BRANCH_W
IN_COLS = QKVG_COLS + N_HEADS + N_BRANCH * D_MODEL
EPS = 1e-6
NEG = -1e30


def rmsnorm(x, g):
    xf = x.astype(jnp.float32)
    y = xf * lax.rsqrt(jnp.mean(xf * xf, axis=-1, keepdims=True) + EPS)
    return (y * g.astype(jnp.float32)).astype(x.dtype)

def to_heads(t):
    b, s, _ = t.shape
    return t.reshape(b, s, N_HEADS, HEAD_DIM).transpose(0, 2, 1, 3)

def from_heads(o):
    b, h, s, d = o.shape
    return o.transpose(0, 2, 1, 3).reshape(b, s, h * d)

def to_blocks(t, size):
    b, h, s, d = t.shape
    return t.reshape(b, h, s // size, size, d).transpose(2, 0, 1, 3, 4)

def from_blocks(o):
    nb, b, h, size, d = o.shape
    return o.transpose(1, 2, 0, 3, 4).reshape(b, h, nb * size, d)

def forgetting_attention(q, k, v, f_logit):
    b, h, s, d = q.shape
    nb = s // Q_BLOCK
    scale = d ** -0.5
    log_f = jax.nn.log_sigmoid(f_logit.astype(jnp.float32))
    c = jnp.cumsum(log_f, axis=1).transpose(0, 2, 1)
    outs = []
    for i in range(nb):
        lo, hi = i * Q_BLOCK, (i + 1) * Q_BLOCK
        logits = jnp.einsum('bhqd,bhkd->bhqk', q[:, :, lo:hi], k[:, :, :hi]).astype(jnp.float32) * scale
        logits = logits + c[:, :, lo:hi, None] - c[:, :, None, :hi]
        mask = jnp.arange(hi)[None, :] <= jnp.arange(lo, hi)[:, None]
        logits = jnp.where(mask, logits, NEG)
        p = jax.nn.softmax(logits, axis=-1).astype(v.dtype)
        outs.append(jnp.einsum('bhqk,bhkd->bhqd', p, v[:, :, :hi]))
    return jnp.concatenate(outs, axis=2)

def chunked_relpos_attention(q, k, v, rel_bias):
    b, h, s, d = q.shape
    nc = s // CHUNK
    scale = d ** -0.5
    pad = LEFT_CHUNKS * CHUNK
    kp = jnp.pad(k, ((0, 0), (0, 0), (pad, 0), (0, 0)))
    vp = jnp.pad(v, ((0, 0), (0, 0), (pad, 0), (0, 0)))
    qi_pos = jnp.arange(CHUNK)
    band_pos = jnp.arange(BAND)
    rel = pad + qi_pos[:, None] - band_pos[None, :]
    idx = jnp.clip(rel, -MAX_REL, MAX_REL) + MAX_REL
    bias = rel_bias[:, idx].astype(jnp.float32)

    def chunk(args):
        qc, ci = args
        start = ci * CHUNK
        kb = lax.dynamic_slice_in_dim(kp, start, BAND, axis=2)
        vb = lax.dynamic_slice_in_dim(vp, start, BAND, axis=2)
        logits = jnp.einsum('bhqd,bhkd->bhqk', qc, kb).astype(jnp.float32) * scale + bias
        valid = (start - pad + band_pos) >= 0
        logits = jnp.where(valid, logits, NEG)
        p = jax.nn.softmax(logits, axis=-1).astype(v.dtype)
        return jnp.einsum('bhqk,bhkd->bhqd', p, vb)

    o = lax.map(chunk, (to_blocks(q, CHUNK), jnp.arange(nc)))
    return from_blocks(o)

def stick_breaking_attention(q, k, v):
    b, h, s, d = q.shape
    nb = s // Q_BLOCK
    scale = d ** -0.5
    ar = jnp.arange(Q_BLOCK)
    upper = (ar[:, None] >= ar[None, :]).astype(jnp.float32)
    hp = lax.Precision.HIGHEST
    outs = []
    for i in range(nb):
        nk = i + 1
        lo, hi = i * Q_BLOCK, nk * Q_BLOCK
        z = jnp.einsum('bhqd,bhkd->bhqk', q[:, :, lo:hi], k[:, :, :hi]).astype(jnp.float32) * scale
        mask = jnp.arange(hi)[None, :] < jnp.arange(lo, hi)[:, None]
        lk = jnp.where(mask, jax.nn.log_sigmoid(-z), 0.0).reshape(b, h, Q_BLOCK, nk, Q_BLOCK)
        r_in = jnp.einsum('bhqnk,kj->bhqnj', lk, upper, precision=hp)
        tot = r_in[..., 0]
        nbk = jnp.arange(nk)
        later_m = (nbk[:, None] > nbk[None, :]).astype(jnp.float32)
        later = jnp.einsum('bhqm,mn->bhqn', tot, later_m, precision=hp)
        r = (r_in + later[..., None]).reshape(b, h, Q_BLOCK, hi)
        a = jnp.where(mask, jnp.exp(z + r), 0.0).astype(v.dtype)
        outs.append(jnp.einsum('bhqk,bhkd->bhqd', a, v[:, :, :hi]))
    return jnp.concatenate(outs, axis=2)

def hybrid_layer(x, norm_g, w_in, b_f, b_gate, qk_norm_g, rel_bias, w_up, w_out):
    b, s, _ = x.shape
    hn = rmsnorm(x, norm_g)
    proj = jnp.einsum('bsd,dc->bsc', hn, w_in)
    br = proj[..., :QKVG_COLS].reshape(b, s, N_BRANCH, 4, BRANCH_W)
    f_logit = proj[..., QKVG_COLS:QKVG_COLS + N_HEADS] + b_f
    gates = jax.nn.sigmoid(proj[..., QKVG_COLS + N_HEADS:] + b_gate).reshape(b, s, N_BRANCH, D_MODEL)

    qa = rmsnorm(to_heads(br[:, :, 0, 0]), qk_norm_g[0])
    ka = rmsnorm(to_heads(br[:, :, 0, 1]), qk_norm_g[1])
    ya = forgetting_attention(qa, ka, to_heads(br[:, :, 0, 2]), f_logit)
    qb = rmsnorm(to_heads(br[:, :, 1, 0]), qk_norm_g[2])
    kb = rmsnorm(to_heads(br[:, :, 1, 1]), qk_norm_g[3])
    yb = chunked_relpos_attention(qb, kb, to_heads(br[:, :, 1, 2]), rel_bias)
    yc = stick_breaking_attention(to_heads(br[:, :, 2, 0]), to_heads(br[:, :, 2, 1]),
                                  to_heads(br[:, :, 2, 2]))

    ys = jnp.stack([from_heads(ya), from_heads(yb), from_heads(yc)], axis=2)
    ys = ys * jax.nn.silu(br[:, :, :, 3])
    up = jnp.einsum('bsnw,nwd->bsnd', ys, w_up)
    merged = jnp.sum(gates * up, axis=2)
    return x + jnp.einsum('bsd,de->bse', merged, w_out)

def second_inputs(seed: int = 0) -> dict:
    key = jax.random.key(seed)
    ks = jax.random.split(key, 10)
    f32 = jnp.float32
    x = jax.random.normal(ks[0], (BATCH, SEQ, D_MODEL), f32)
    norm_g = 1.0 + 0.02 * jax.random.normal(ks[1], (DEPTH, D_MODEL), f32)
    w_in = jax.random.normal(ks[2], (DEPTH, D_MODEL, IN_COLS), f32) * D_MODEL ** -0.5
    b_f = 3.0 + 0.1 * jax.random.normal(ks[3], (DEPTH, N_HEADS), f32)
    b_gate = 0.02 * jax.random.normal(ks[4], (DEPTH, N_BRANCH * D_MODEL), f32)
    qk_norm_g = 1.0 + 0.02 * jax.random.normal(ks[5], (DEPTH, 4, HEAD_DIM), f32)
    rel_bias = 0.5 * jax.random.normal(ks[6], (DEPTH, N_HEADS, N_REL), f32)
    w_up = jax.random.normal(ks[7], (DEPTH, N_BRANCH, BRANCH_W, D_MODEL), f32) * BRANCH_W ** -0.5
    w_out = jax.random.normal(ks[8], (DEPTH, D_MODEL, D_MODEL), f32) * D_MODEL ** -0.5
    return {"x": x, "norm_g": norm_g, "w_in": w_in, "b_f": b_f, "b_gate": b_gate,
            "qk_norm_g": qk_norm_g, "rel_bias": rel_bias, "w_up": w_up, "w_out": w_out}

def second_block(x, norm_g, w_in, b_f, b_gate, qk_norm_g, rel_bias, w_up, w_out):
    for layer in range(DEPTH):
        x = hybrid_layer(x, norm_g[layer], w_in[layer], b_f[layer], b_gate[layer],
                         qk_norm_g[layer], rel_bias[layer], w_up[layer], w_out[layer])
    return x


def setup_inputs(seed=0):
    out = dict(first_inputs(seed))
    for name, value in second_inputs(seed + 1).items():
        if name != "x":
            out[name + "_2"] = value
    return out


def reference(
    x, mem, w_in, b_gate, kv_norm_g, idx_k_norm_g, idx_k_norm_b, w_uk, w_uv, w_o_dsa, w_o_moba,
    w_out, w_q_mem, w_kv_mem, w_o_mem, w_ffn_in, w_ffn_out, ln_g, ln_b, norm_g_2, w_in_2, b_f_2,
    b_gate_2, qk_norm_g_2, rel_bias_2, w_up_2, w_out_2,
):
    x = first_block(
        x, mem, w_in, b_gate, kv_norm_g, idx_k_norm_g, idx_k_norm_b, w_uk, w_uv, w_o_dsa,
        w_o_moba, w_out, w_q_mem, w_kv_mem, w_o_mem, w_ffn_in, w_ffn_out, ln_g, ln_b,
    )
    return second_block(
        x, norm_g_2, w_in_2, b_f_2, b_gate_2, qk_norm_g_2, rel_bias_2, w_up_2, w_out_2,
    )


_drawn_inputs = setup_inputs


def setup_inputs(seed=0):
    import zlib

    import numpy as np

    out = dict(_drawn_inputs(seed))
    spreads = {}
    factors = {'b_gate': 8.0,
     'kv_norm_g': 8.0,
     'idx_k_norm_g': 8.0,
     'idx_k_norm_b': 8.0,
     'norm_g_2': 7.067,
     'b_f_2': 64.0,
     'b_gate_2': 8.0,
     'qk_norm_g_2': 8.0}
    for name, (base, spread) in spreads.items():
        noise = np.random.default_rng([zlib.crc32(name.encode()), seed]).standard_normal(out[name].shape)
        drawn = base * np.exp(spread * noise) if base else spread * noise
        out[name] = __import__('jax').numpy.asarray(drawn.astype(out[name].dtype))
    for name, factor in factors.items():
        out[name] = (out[name] * factor).astype(out[name].dtype)
    return out
```

```python
from contextlib import ExitStack, contextmanager

import concourse.bass as bass
from concourse import mybir

F32 = mybir.dt.float32
F32R = mybir.dt.float32r
ACT = mybir.ActivationFunctionType
ALU = mybir.AluOpType
AX = mybir.AxisListType
ds = bass.ds

P = 128
S = 256
R = S // P
D = 2048
KT = D // P
HD = 128
NB = 512
GK = 2
SLOTS = 4
AHEAD = 2
H_DSA, H_MOBA, H_MEM, H_B2 = 8, 8, 4, 4
LAT, IDX_H, IDX_D = 256, 16, 64
TOPK = S // 4
D_FF = -(-8 * D // (3 * 256)) * 256
BR_W = H_B2 * HD
MAX_REL = 128
CHUNK = 64
ALPHA = 2.0 ** 0.25
SCALE = HD ** -0.5
LN_EPS = 1e-5
EPS = 1e-6
NEG = -1e30
TAKEN = -3e38
CW = P + S
TILE_COLS = ((0, P), (P, CW))

C_QDSA = 0
C_LAT = C_QDSA + H_DSA * HD
C_QIDX = C_LAT + LAT
C_KIDX = C_QIDX + IDX_H * IDX_D
C_QM = C_KIDX + IDX_D + IDX_H
C_VM = C_QM + 2 * H_MOBA * HD
C_GA = C_VM + H_MOBA * HD
C_GB = C_GA + D
C_F = 3 * 4 * BR_W
C_G2 = C_F + H_B2
KIDX_W = IDX_D + IDX_H
FFN_PARTS = ((0, 4), (4, 4), (8, 3))
N_GROUPS = (
    2 * KT // GK + (2 + 2 + 4 + 2) * KT // GK + 2 * 4 * (KT // GK + 8 // GK) + 4 * KT // GK
    + 2 * KT // GK + KT // GK + 4 * 4 // GK + 2 * (D_FF // NB) * KT // GK + 4 * D_FF // P // GK
    + 3 * (4 * KT // GK + 4 * KT // GK + 4 * 4 // GK) + 4 * KT // GK
)


TOKENS = {
    "pe": ("s_done", "t_done", "x_done", "o_done"),
    "act": ("x_ready", "pt_ready", "idx_read"),
    "dve": ("s_read", "o_free", "relu_used"),
}


class Counts:

    def __init__(self, engine, per):
        self.engine, self.per, self.local, self.loop_at = engine, per, {}, None
        self.base = {name: 1 for names in TOKENS.values() for name in names}

    def value(self, name, back=0):
        fixed = self.base.get(name, 0) + self.local.get(name, 0) - back
        if self.loop_at is None:
            return fixed
        i, key = self.loop_at
        step = self.per.get((key, name), 0)
        assert fixed > 0 or step == 0 or self.per.get("counting"), (key, name, fixed)
        return fixed + i * step if step else fixed

    def next(self, name, n=1):
        self.local[name] = self.local.get(name, 0) + n
        return self.value(name)

    def mark(self, mark, name):
        self.per[("mark", mark)] = self.value(name)

    def at(self, mark):
        return self.per.get(("mark", mark), 1)

    @contextmanager
    def loop(self, eng, name, n):
        for k, v in self.local.items():
            self.base[k] = self.base.get(k, 0) + v
        self.local = {}
        key = (self.engine, name)
        with eng.Fori(0, n) as i:
            self.loop_at = (i, key)
            yield i
        self.loop_at = None
        for k, v in self.local.items():
            if self.per.get("counting"):
                self.per[(key, k)] = v
            assert self.per[(key, k)] == v
            self.base[k] = self.base.get(k, 0) + n * v
        self.local = {}


def some(value):
    return not isinstance(value, int) or value > 0


def two_blocks(nc, a, out, per):
    ctx = ExitStack()
    with ctx:
        def sb(name, shape, dt=F32):
            return ctx.enter_context(nc.sbuf_tensor("b_" + name, shape, dt))

        sems = {}

        def sem(name):
            if name not in sems:
                sems[name] = ctx.enter_context(nc.semaphore("s_" + name))
            return sems[name]

        stage = sb("stage", [P, SLOTS, GK, NB])
        w_hi = sb("w_hi", [P, SLOTS, GK, NB], F32R)
        w_lo = sb("w_lo", [P, SLOTS, GK, NB], F32R)
        x_hi = sb("x_hi", [P, KT, S], F32R)
        x_lo = sb("x_lo", [P, KT, S], F32R)
        vec_a = sb("vec_a", [P, D])
        vec_b = sb("vec_b", [P, D])
        ident = sb("ident", [P, P])
        ones = sb("ones", [P, P])
        causal = sb("causal", [P, CW])
        strict_t = sb("strict_t", [P, CW])
        lower = sb("lower", [P, P])
        nat = sb("nat", [P, R, NB])
        logits = sb("logits", [P, 2, NB])
        probs_t = sb("probs_t", [P, NB])
        aux_a = sb("aux_a", [P, NB])
        aux_b = sb("aux_b", [P, NB])
        q_st = sb("q_st", [P, S])
        v_st = sb("v_st", [P, R, HD])
        best8 = sb("best8", [P, 8])
        qk_g = sb("qk_g", [P, 4])
        bf_v = sb("bf_v", [P, H_B2])
        logf = sb("logf", [P, R, H_B2])
        f_a = sb("f_a", [P, R, H_B2])
        f_b = sb("f_b", [P, R, H_B2])
        c_q = sb("c_q", [P, R, H_B2])
        stats = sb("stats", [P, R, 4, 6])
        mv = sb("mv", [P, R, 2])
        sd = sb("sd", [P, R * 4])
        rstd = sb("rstd", [P, R * 4])
        ssq = sb("ssq", [P, R * 4])
        nmax = sb("nmax", [P, R])
        rsum = sb("rsum", [P, R])
        rinv = sb("rinv", [P, R])

        def shared(*shapes):
            with ExitStack() as own:
                return [own.enter_context(nc.sbuf_tensor("b_" + n, s, t)) for n, s, t in shapes]

        (qi_st, relu_s, score, lat_nat, lat_t, kidx2, kidx_t, w_uk_st, w_uv_st, bias_d, bias_m, w_idx, kv_g,
         ik_g, ik_b) = shared(
            ("qi_st", [P, 2, S], F32),
            ("relu_s", [P, CW], F32),
            ("score", [P, CW], F32),
            ("lat_nat", [P, R, LAT], F32),
            ("lat_t", [P, 2, S], F32),
            ("kidx2", [P, R, 2 * IDX_D], F32),
            ("kidx_t", [P, S], F32),
            ("w_uk_st", [P, LAT], F32),
            ("w_uv_st", [P, 2, HD], F32),
            ("bias_d", [P, CW], F32),
            ("bias_m", [P, CW], F32),
            ("w_idx", [P, R, IDX_H], F32),
            ("kv_g", [P, LAT], F32),
            ("ik_g", [P, IDX_D], F32),
            ("ik_b", [P, IDX_D], F32),
        )
        bias4 = sb("bias4", [P, H_B2, CW], F32)
        silu_g = sb("silu_g", [P, R, NB], F32)
        upto = sb("upto", [P, R, S], F32)
        wf = sb("wf", [P, KT, H_B2], F32)
        wf_hi = sb("wf_hi", [P, KT, H_B2], F32R)
        wf_lo = sb("wf_lo", [P, KT, H_B2], F32R)
        g_col = sb("g_col", [P, KT], F32)
        sb("pad_small", [P, 1280])
        (qkm_t, vm, qi_t, qd_t, oh, ol, gate_a) = shared(
            ("qkm_t", [P, 2 * H_MOBA, S], F32), ("vm", [P, R, H_MOBA * HD], F32),
            ("qi_t", [P, IDX_H // 2, S], F32), ("qd_t", [P, H_DSA, S], F32),
            ("oh", [P, H_DSA, S], F32R), ("ol", [P, H_DSA, S], F32R), ("gate_a", [P, R, D], F32))
        (_, gate_b) = shared(("pad", [P, 3 * 8 * S], F32), ("gate_b", [P, R, D], F32))
        x_res = sb("x_res", [P, R, D])
        (mem_nat, mem_hi, mem_lo, kmem_t, vmem) = shared(
            ("mem_nat", [P, R, D], F32), ("mem_hi", [P, KT, S], F32R), ("mem_lo", [P, KT, S], F32R),
            ("kmem_t", [P, H_MEM, S], F32), ("vmem", [P, R, H_MEM * HD], F32))
        (qmem_t, om_h, om_l) = shared(
            ("qmem_t", [P, H_MEM, S], F32), ("om_h", [P, H_MEM, S], F32R), ("om_l", [P, H_MEM, S], F32R))
        (ff_h, ff_l) = shared(("ff_h", [P, 4 * 4, S], F32R), ("ff_l", [P, 4 * 4, S], F32R))
        (q2_t, k2_t, v2, s2_t, y_h, y_l, gate2, merged2) = shared(
            ("q2_t", [P, H_B2, S], F32), ("k2_t", [P, H_B2, S], F32), ("v2", [P, R, BR_W], F32),
            ("s2_t", [P, H_B2, S], F32), ("y_h", [P, H_B2, S], F32R), ("y_l", [P, H_B2, S], F32R),
            ("gate2", [P, R, D], F32), ("merged2", [P, R, D], F32))
        x_in = gate_a
        ps = ctx.enter_context(nc.psum_tensor("b_ps", [P, 8, NB], F32))
        ACC, TP, SC, AUX, PT, OT = 0, 2, 4, 5, 6, 7
        ext = nc.dram_tensor("rel_ext", [H_B2, 2 * S - 1], F32).ap()
        block = ctx.enter_context(nc.Block())

        def flat(x):
            return x.rearrange("p a n -> p (a n)")

        def width(g):
            return NB if not isinstance(g, int) or g >= 2 * KT // GK else (KIDX_W, LAT)[g // (KT // GK)]


        @block.sync
        def _(sp):
            c = Counts("sp", per)

            def group(w, row, col, n=NB):
                slot = c.local.get("g", 0) + (c.base.get("g", 0))
                slot %= SLOTS
                back = c.value("g", SLOTS - 1)
                if some(back):
                    sp.wait_ge(sem("lo_done"), back)
                src = w[row:row + GK * P, ds(col, n)].rearrange("(t p) n -> p t n", p=P)
                sp.dma_start(stage[:, slot, :, 0:n], src).then_inc(sem(f"landed{slot}"), 16)
                c.next("g")

            def blockw(w, row, col, kts=KT, n=NB):
                for j in range(kts // GK):
                    group(w, row + j * GK * P, col, n)

            def blocks(name, w, row, col, count, kts=KT):
                with c.loop(sp, name, count) as i:
                    blockw(w, row, col + i * NB, kts)

            blockw(a["w_in"], 0, C_KIDX, n=KIDX_W)
            blockw(a["w_in"], 0, C_LAT, n=LAT)
            blocks("q_idx", a["w_in"], 0, C_QIDX, 2)
            blocks("q_dsa", a["w_in"], 0, C_QDSA, 2)
            blocks("qk_m", a["w_in"], 0, C_QM, 4)
            for b in range(2):
                blockw(a["w_in"], 0, C_VM + b * NB)
            for gcol, wo in ((C_GA, a["w_o_dsa"]), (C_GB, a["w_o_moba"])):
                blocks(f"gate{gcol}", a["w_in"], 0, gcol, 4)
                blocks(f"up{gcol}", wo, 0, 0, 4, 8)
            blocks("w_out", a["w_out"], 0, 0, 4)
            for b in range(2):
                blockw(a["w_kv_mem"], 0, b * NB)
            blockw(a["w_q_mem"], 0, 0)
            for b in range(4):
                blockw(a["w_o_mem"], 0, b * NB, 4)
            for f0, nf in FFN_PARTS:
                with c.loop(sp, f"ffn_in{f0}", nf) as i:
                    blockw(a["w_ffn_in"], 0, (i + f0) * NB)
                    blockw(a["w_ffn_in"], 0, (i + f0) * NB + D_FF)
                if nf == 4:
                    blocks(f"ffn_out{f0}", a["w_ffn_out"], f0 * NB, 0, 4, 4 * nf)
                else:
                    with c.loop(sp, f"ffn_out{f0}", 2) as i:
                        for b in range(2):
                            blockw(a["w_ffn_out"], f0 * NB, (i * 2 + b) * NB, 4 * nf)
            for n in range(3):
                for b in range(4):
                    blockw(a["w_in_2"], 0, (4 * n + (0, 1, 3, 2)[b]) * BR_W)
                blocks(f"gate2_{n}", a["w_in_2"], 0, C_G2 + n * D, 4)
                with c.loop(sp, f"up2_{n}", 2) as i:
                    for b in range(2):
                        blockw(a["w_up_2"], n * BR_W, (i * 2 + b) * NB, 4)
            for b in range(4):
                blockw(a["w_out_2"], 0, b * NB)
            assert c.value("g") == N_GROUPS, (c.value("g"), N_GROUPS)
            for b in range(4):
                sp.wait_ge(sem("tile_out1"), c.at(f"final{b}"))
                sp.dma_start(out[:, b * NB:(b + 1) * NB].rearrange("(r p) n -> p r n", p=P),
                             x_res[:, :, b * NB:(b + 1) * NB]).then_inc(sem("out"), 16)
            sp.wait_ge(sem("out"), 16 * 4)

        @block.gpsimd
        def _(pool):
            c = Counts("pool", per)

            def load(dst, src, name, **how):
                pool.dma_start(dst, src, **how).then_inc(sem(name), 16)

            def rows(v):
                return v.partition_broadcast(P)

            load(x_in[:, :, :], a["x"].rearrange("(r p) n -> p r n", p=P), "x_in")
            load(kv_g[:, :], rows(a["kv_norm_g"]), "small")
            load(ik_g[:, :], rows(a["idx_k_norm_g"]), "small")
            load(ik_b[:, :], rows(a["idx_k_norm_b"]), "small")
            load(vec_a[:, :], rows(a["b_gate"][0, :]), "vec")
            load(vec_b[:, :], rows(a["b_gate"][1, :]), "vec")
            load(w_uk_st[:, :], a["w_uk"][0:HD, :], "uk")
            load(w_uv_st[:, :, :], a["w_uv"][0:LAT, :].rearrange("(t p) n -> p t n", p=P), "uv")
            pool.memset(ident[:, :], 0.0).then_inc(sem("pool_step"), 1)
            pool.wait_ge(sem("pool_step"), c.next("pool_step"))
            pool.affine_select(out=ident[:, :], in_=ident[:, :], compare_op=ALU.not_equal, fill=1.0,
                               base=0, pattern=[[-1, P]], channel_multiplier=1).then_inc(sem("pool_step"), 1)
            pool.wait_ge(sem("pool_step"), c.next("pool_step"))
            pool.memset(ones[:, :], 1.0).then_inc(sem("pool_step"), 1)
            pool.wait_ge(sem("pool_step"), c.next("pool_step"))
            pool.memset(causal[:, :], 0.0).then_inc(sem("pool_step"), 1)
            pool.wait_ge(sem("pool_step"), c.next("pool_step"))
            pool.memset(strict_t[:, :], 0.0).then_inc(sem("pool_step"), 1)
            pool.wait_ge(sem("pool_step"), c.next("pool_step"))
            pool.memset(lower[:, :], 1.0).then_inc(sem("pool_step"), 1)
            pool.wait_ge(sem("pool_step"), c.next("pool_step"))
            pool.iota(bias_m[:, 0:P], pattern=[[1, P]], base=0, channel_multiplier=-1,
                      allow_small_or_imprecise_dtypes=True).then_inc(sem("pool_step"), 1)
            pool.wait_ge(sem("pool_step"), c.next("pool_step"))
            pool.iota(bias_m[:, P:CW], pattern=[[1, S]], base=-P, channel_multiplier=-1,
                      allow_small_or_imprecise_dtypes=True).then_inc(sem("pool_step"), 1)
            pool.wait_ge(sem("pool_step"), c.next("pool_step"))
            for t, (lo, hi) in enumerate(TILE_COLS):
                pool.affine_select(out=causal[:, lo:hi], in_=causal[:, lo:hi], compare_op=ALU.is_ge,
                                   fill=NEG, base=t * P, pattern=[[-1, hi - lo]], channel_multiplier=1)\
                    .then_inc(sem("pool_step"), 1)
                pool.wait_ge(sem("pool_step"), c.next("pool_step"))
                pool.affine_select(out=bias_m[:, lo:hi], in_=bias_m[:, lo:hi], compare_op=ALU.is_ge,
                                   fill=NEG, base=t * P, pattern=[[-1, hi - lo]], channel_multiplier=1)\
                    .then_inc(sem("pool_step"), 1)
                pool.wait_ge(sem("pool_step"), c.next("pool_step"))
            for t, (lo, hi) in enumerate(((0, S), (S, CW))):
                pool.affine_select(out=strict_t[:, lo:hi], in_=strict_t[:, lo:hi], compare_op=ALU.is_gt,
                                   fill=NEG, base=0, pattern=[[1, hi - lo]], channel_multiplier=-1)\
                    .then_inc(sem("pool_step"), 1)
                pool.wait_ge(sem("pool_step"), c.next("pool_step"))
            pool.affine_select(out=lower[:, :], in_=lower[:, :], compare_op=ALU.is_ge, fill=0.0,
                               base=0, pattern=[[-1, P]], channel_multiplier=1).then_inc(sem("pool_step"), 1)
            pool.wait_ge(sem("pool_step"), c.next("pool_step"))
            pool.memset(score[:, :], 0.0).then_inc(sem("const"), 1)

            side = S - 1 - MAX_REL
            row = gate_b[0:H_B2, 0, 0:2 * S - 1]
            load(row[:, side:side + 2 * MAX_REL + 1], a["rel_bias"], "ext")
            pool.wait_ge(sem("ext"), 16)
            for edge, at in ((row[:, 0:side], side), (row[:, side + 2 * MAX_REL + 1:], side + 2 * MAX_REL)):
                pool.tensor_copy(edge, row[:, at:at + 1].to_broadcast([H_B2, side])).then_inc(sem("pool_step"), 1)
                pool.wait_ge(sem("pool_step"), c.next("pool_step"))
            load(ext, row, "ext")

            pool.wait_ge(sem("tp_free"), c.at("q_idx"))
            pool.tensor_copy(qi_st[:, :, :], qi_t[:, 0:2, :]).then_inc(sem("qi_staged"), 1)
            with c.loop(pool, "qk_m", 3) as i:
                pool.wait_ge(sem("idx_done"), c.next("idx_done", 4))
                pool.tensor_copy(qi_st[:, :, :], qi_t[:, ds(i * 2 + 2, 2), :]).then_inc(sem("qi_staged"), 1)

            with c.loop(pool, "dsa", H_DSA - 1) as i:
                pool.wait_ge(sem("x_done"), c.next("x_done"))
                load(w_uk_st[:, :], a["w_uk"][ds((i + 1) * HD, HD), :], "uk")
                c.next("x_done")
                pool.wait_ge(sem("o_done"), c.next("o_done"))
                load(w_uv_st[:, :, :], a["w_uv"][ds((i + 1) * LAT, LAT), :].rearrange("(t p) n -> p t n", p=P),
                     "uv")

            def stage_heads(name, n, q_src, v_src):
                with c.loop(pool, name, n) as i:
                    pool.wait_ge(sem("s_done"), i + c.at(name + "s"))
                    pool.tensor_copy(q_st[:, :], flat(q_src[:, ds(i, 1), :])).then_inc(sem("q_staged"), 1)
                    pool.wait_ge(sem("o_done"), i + c.at(name + "o"))
                    pool.tensor_copy(v_st[:, :, :], v_src[:, :, ds(i * HD, HD)]).then_inc(sem("v_staged"), 1)

            stage_heads("moba", H_MOBA, qkm_t[:, 0:H_MOBA, :], vm)
            pool.wait_ge(sem("tile_out1"), c.at("merged"))
            load(x_res[:, :, :], a["x"].rearrange("(r p) n -> p r n", p=P), "x_res")
            load(vec_a[:, :], rows(a["ln_g"][0, :]), "vec")
            load(vec_b[:, :], rows(a["ln_b"][0, :]), "vec")
            pool.wait_ge(sem("tp_free"), c.at("fed"))
            load(mem_nat[:, :, :], a["mem"].rearrange("(r p) n -> p r n", p=P), "mem")
            load(g_col[:, :], a["norm_g"].rearrange("(t p) -> p t", p=P), "small2",
                 allow_slow_non_contiguous=True)
            load(qk_g[:, :], a["qk_norm_g"].rearrange("n p -> p n"), "small2",
                 allow_slow_non_contiguous=True)
            load(bf_v[:, :], rows(a["b_f"]), "small2")
            load(wf[:, :, :], a["w_in_2"][:, C_F:C_F + H_B2].rearrange("(t p) n -> p t n", p=P), "small2")
            pool.memset(upto[:, :, :], 1.0).then_inc(sem("pool_step"), 1)
            pool.wait_ge(sem("pool_step"), c.next("pool_step"))
            for t in range(R):
                pool.affine_select(out=upto[:, t, :], in_=upto[:, t, :], compare_op=ALU.is_ge, fill=0.0,
                                   base=-t * P, pattern=[[1, S]], channel_multiplier=-1).then_inc(sem("pool_step"), 1)
                pool.wait_ge(sem("pool_step"), c.next("pool_step"))
            for n in (1, 2):
                pool.wait_ge(sem("chunk"), c.at(f"normed{n}"))
                load(vec_a[:, :], rows(a["ln_g"][n, :]), "vec")
                load(vec_b[:, :], rows(a["ln_b"][n, :]), "vec")
            pool.wait_ge(sem("chunk3"), 4)
            load(vec_a[:, :], rows(a["b_gate_2"][0, 0:D]), "vec")
            pool.wait_ge(sem("ext"), 32)
            for n in range(3):
                pool.wait_ge(sem("tp_free"), c.at(f"q2_{n}"))
                pool.wait_ge(sem("tile_out1"), c.at(f"v2_{n}"))
                stage_heads(f"branch{n}", H_B2, q2_t if n < 2 else k2_t, v2)
                if n < 2:
                    pool.wait_ge(sem("tile_out1"), c.at(f"gates2_{n}"))
                    load(vec_a[:, :], rows(a["b_gate_2"][0, (n + 1) * D:(n + 2) * D]), "vec")
                if n == 0:
                    pool.wait_ge(sem("s_read"), c.at("forget"))
                    for h in range(H_B2):
                        for lo, hi in TILE_COLS:
                            src = bass.AP(tensor=ext.tensor, offset=ext.offset + h * (2 * S - 1) + P,
                                          ap=[[1, P], [1, hi - lo]])
                            load(bias4[:, h, lo:hi], src, "rel")

        @block.tensor
        def _(pe):
            c = Counts("pe", per)
            mm, T = nc.tensor.matmul, nc.tensor.transpose

            def group(kt, first, last, hi, lo, n=NB):
                slot = (c.base.get("g", 0) + c.local.get("g", 0)) % SLOTS
                pe.wait_ge(sem("lo_done"), c.next("lo_done"))
                for r in range(R):
                    if first and some(c.value(f"tile_out{r}")):
                        pe.wait_ge(sem(f"tile_out{r}"), c.value(f"tile_out{r}"))
                    for t in range(GK):
                        rows = slice(r * P, (r + 1) * P)
                        for k, (x, w) in enumerate(((hi, w_hi), (hi, w_lo), (lo, w_hi))):
                            ins = mm(ps[:, ACC + r, 0:n], x[:, kt + t, rows], w[:, slot, t, 0:n],
                                     start=first and t == 0 and k == 0, stop=last and t == GK - 1 and k == 2)
                    if r == 1:
                        ins.then_inc(sem("w_used"), 1)
                    elif last:
                        ins.then_inc(sem("tile0_done"), 1)
                c.next("g")

            def weights(kts=KT, hi=x_hi, lo=x_lo, n=NB, kt0=0, hook=None):
                groups = kts // GK
                for j in range(groups):
                    group(kt0 + j * GK, j == 0, j == groups - 1, hi, lo, n)
                    if hook:
                        hook(j)
                for r in range(R):
                    c.next(f"tile_out{r}")

            def turn(ready, width=4):
                pe.wait_ge(sem("tp_free"), c.value("tp_free"))
                for r in range(R):
                    ready(r)
                    for j in range(4):
                        ins = T(ps[:, TP + j // 2, (j % 2) * S + r * P:(j % 2) * S + (r + 1) * P],
                                nat[:, r, j * P:(j + 1) * P], ident[:, :])
                        if r == 1 and j % 2:
                            ins.then_inc(sem("tp_done"), 1)
                c.next("tp_free", 2)

            def left(r):
                pe.wait_ge(sem(f"tile_out{r}"), c.value(f"tile_out{r}"))

            def nat_ready(r):
                if r == 0:
                    pe.wait_ge(sem("nat_ready"), c.next("nat_ready"))

            def feed(src, ready):
                for t in range(KT // 2):
                    ready(t)
                    if some(c.value("tp_free", 1)):
                        pe.wait_ge(sem("tp_free"), c.value("tp_free", 1))
                    for kk in range(2):
                        for r in range(R):
                            ins = T(ps[:, TP + t % 2, kk * S + r * P:kk * S + (r + 1) * P],
                                    src[:, r, (2 * t + kk) * P:(2 * t + kk + 1) * P], ident[:, :])
                    ins.then_inc(sem("tp_done"), 1)
                    c.next("tp_free")
                pe.wait_ge(sem("tp_free"), c.value("tp_free"))

            def by_chunk(t):
                if t % 2 == 0:
                    pe.wait_ge(sem("chunk"), c.next("chunk"))

            def scores(pairs):
                pe.wait_ge(sem("s_read"), c.value("s_read"))
                for t, (lo, hi) in enumerate(TILE_COLS):
                    for k, (q, keys) in enumerate(pairs):
                        ins = mm(ps[:, SC, lo:hi], q[:, t * P:(t + 1) * P], keys(hi - lo),
                                 start=k == 0, stop=k == len(pairs) - 1)
                ins.then_inc(sem("s_done"), 1)
                c.next("s_read")

            def turn_probs():
                pe.wait_ge(sem("p_ready"), c.next("p_ready"))
                pe.wait_ge(sem("pt_ready"), c.value("pt_ready"))
                for j in range(3):
                    ins = T(ps[:, PT, j * P:(j + 1) * P], logits[:, 0, j * P:(j + 1) * P], ident[:, :])
                ins.then_inc(sem("t_done"), 1)
                c.next("pt_ready")

            def weigh(bank, col, v0, v1):
                mm(ps[:, bank, col:col + S], v0, probs_t[:, 0:S], start=True, stop=False)
                return mm(ps[:, bank, col + P:col + S], v1, probs_t[:, S:CW], start=False, stop=True)

            def outputs():
                pe.wait_ge(sem("pt_ready"), c.value("pt_ready"))
                pe.wait_ge(sem("o_free"), c.value("o_free"))
                pe.wait_ge(sem("v_staged"), c.next("v_staged"))
                weigh(OT, 0, v_st[:, 0, :], v_st[:, 1, :]).then_inc(sem("o_done"), 1)
                c.next("o_free")

            for name in TOKENS["pe"]:
                pe.nop().then_inc(sem(name), 1)
            pe.wait_ge(sem("const"), 1)
            pe.wait_ge(sem("x_in"), 16)
            feed(x_in, lambda t: None)
            weights(n=KIDX_W)
            weights(n=LAT)
            with c.loop(pe, "q_idx", 2):
                weights()
                turn(left)
            pe.wait_ge(sem("tp_free"), c.value("tp_free"))
            pe.wait_ge(sem("nat_ready"), c.next("nat_ready", 2))
            for r in range(R):
                T(ps[:, TP, r * P:(r + 1) * P], kidx2[:, r, :], ident[:, :])
            T(ps[:, TP, S:S + P], kidx2[:, 0, :], ident[:, :]).then_inc(sem("tp_done"), 1)
            for r in range(R):
                for ct in range(2):
                    ins = T(ps[:, TP + 1, ct * S + r * P:ct * S + (r + 1) * P],
                            lat_nat[:, r, ct * P:(ct + 1) * P], ident[:, :])
            ins.then_inc(sem("tp_done"), 1)
            c.next("tp_free", 2)
            with c.loop(pe, "q_dsa", 2):
                weights()
                turn(left)
            with c.loop(pe, "qk_m", 4):
                pe.wait_ge(sem("qi_staged"), c.next("qi_staged"))

                def index_head(j):
                    if j % 2 == 0:
                        return
                    n = j // 2
                    half = slice((n % 2) * IDX_D, (n % 2 + 1) * IDX_D)
                    pe.wait_ge(sem("idx_read"), c.value("idx_read"))
                    for t, (lo, hi) in enumerate(TILE_COLS):
                        ins = mm(ps[:, AUX, lo:hi], qi_st[half, n // 2, t * P:(t + 1) * P],
                                 kidx_t[half, 0:hi - lo], start=True, stop=True)
                    ins.then_inc(sem("idx_done"), 1)
                    c.next("idx_read")
                weights(hook=index_head)
                turn(left)
            for b in range(2):
                weights()
            pe.wait_ge(sem("idx_read"), c.value("idx_read"))

            with c.loop(pe, "dsa", 4) as i:
                def query_latent(h):
                    pe.wait_ge(sem("uk"), c.next("uk", 16))
                    pe.wait_ge(sem("x_ready"), c.value("x_ready"))
                    for ct in range(2):
                        ins = mm(ps[:, AUX, ct * S:(ct + 1) * S], w_uk_st[:, ct * P:(ct + 1) * P],
                                 qd_t[:, ds(h, 1), :], start=True, stop=True)
                    ins.then_inc(sem("x_done"), 1)
                    c.next("x_ready")

                def lat_scores():
                    pe.wait_ge(sem("x_ready"), c.value("x_ready"))
                    scores([(aux_a[:, ct * S:(ct + 1) * S], lambda n, ct=ct: lat_t[:, ct, 0:n])
                            for ct in range(2)])

                def lat_outputs():
                    pe.wait_ge(sem("pt_ready"), c.value("pt_ready"))
                    pe.wait_ge(sem("x_ready"), c.value("x_ready"))
                    for ct in range(2):
                        ins = weigh(AUX, ct * S, lat_nat[:, 0, ct * P:(ct + 1) * P],
                                    lat_nat[:, 1, ct * P:(ct + 1) * P])
                    ins.then_inc(sem("x_done"), 1)
                    c.next("x_ready")

                def value_up():
                    pe.wait_ge(sem("uv"), c.next("uv", 16))
                    pe.wait_ge(sem("x_ready"), c.value("x_ready"))
                    pe.wait_ge(sem("o_free"), c.value("o_free"))
                    for ct in range(2):
                        ins = mm(ps[:, OT, 0:S], w_uv_st[:, ct, :], aux_b[:, ct * S:(ct + 1) * S],
                                 start=ct == 0, stop=ct == 1)
                    ins.then_inc(sem("o_done"), 1)
                    c.next("o_free")

                def dsa(j):
                    if j == 0:
                        query_latent(i * 2)
                    elif j == 1:
                        lat_scores()
                    elif j == 2:
                        query_latent(i * 2 + 1)
                    elif j == 3:
                        turn_probs()
                    elif j == 4:
                        lat_outputs()
                        lat_scores()
                    elif j == 5:
                        value_up()
                    elif j == 6:
                        turn_probs()
                    elif j == 7:
                        lat_outputs()
                        value_up()
                weights(hook=dsa)
            pe.wait_ge(sem("o_free"), c.value("o_free"))
            with c.loop(pe, "up_a", 4):
                weights(kts=8, hi=oh, lo=ol)
            km_t = qkm_t[:, H_MOBA:, :]
            with c.loop(pe, "moba", 4) as i:
                def head_scores(h, keys):
                    pe.wait_ge(sem("q_staged"), c.next("q_staged"))
                    scores([(q_st, lambda n: keys[:, ds(h, 1), 0:n])])

                def moba(j):
                    if j in (0, 3):
                        head_scores(i * 2 + (j == 3), km_t)
                    if j in (2, 5):
                        turn_probs()
                    if j in (3, 6):
                        outputs()
                def moba_ordered(j):
                    if j == 3:
                        outputs()
                        head_scores(i * 2 + 1, km_t)
                    else:
                        moba(j)
                weights(hook=moba_ordered)
            pe.wait_ge(sem("o_free"), c.value("o_free"))
            with c.loop(pe, "up_b", 4):
                weights(kts=8, hi=oh, lo=ol)
            for r in range(R):
                pe.wait_ge(sem(f"tile_out{r}"), c.value(f"tile_out{r}"))
            pe.wait_ge(sem("summed"), c.at("summed1"))
            feed(gate_a, lambda t: None)
            with c.loop(pe, "w_out", 4):
                weights()

            pe.wait_ge(sem("mem"), 16)
            feed(mem_nat, lambda t: None)
            weights(hi=mem_hi, lo=mem_lo)
            turn(left)
            weights(hi=mem_hi, lo=mem_lo)
            feed(x_res, by_chunk)
            weights()
            turn(left)
            pe.wait_ge(sem("tp_free"), c.value("tp_free"))
            for r in range(R):
                pe.wait_ge(sem(f"tile_out{r}"), c.value(f"tile_out{r}"))

            def mem_scores(h):
                pe.wait_ge(sem("s_read"), c.value("s_read", 1))
                for r in range(R):
                    ins = mm(ps[:, SC + h % 2, r * S:(r + 1) * S], qmem_t[:, h, r * P:(r + 1) * P],
                             kmem_t[:, h, :], start=True, stop=True)
                ins.then_inc(sem("s_done"), 1)
                c.next("s_read")

            mem_scores(0)
            for h in range(H_MEM):
                if h + 1 < H_MEM:
                    mem_scores(h + 1)
                pe.wait_ge(sem("p_ready"), c.next("p_ready"))
                pe.wait_ge(sem("pt_ready"), c.value("pt_ready"))
                for kt in range(2):
                    for r in range(R):
                        ins = T(ps[:, PT, kt * S + r * P:kt * S + (r + 1) * P],
                                logits[:, h % 2, r * S + kt * P:r * S + (kt + 1) * P], ident[:, :])
                ins.then_inc(sem("t_done"), 1)
                pe.wait_ge(sem("pt_ready"), c.next("pt_ready"))
                pe.wait_ge(sem("o_free"), c.value("o_free"))
                for kt in range(2):
                    ins = mm(ps[:, OT, 0:S], vmem[:, kt, h * HD:(h + 1) * HD],
                             probs_t[:, kt * S:(kt + 1) * S], start=kt == 0, stop=kt == 1)
                ins.then_inc(sem("o_done"), 1)
                c.next("o_free")
            pe.wait_ge(sem("o_free"), c.value("o_free"))
            for b in range(4):
                weights(kts=4, hi=om_h, lo=om_l)
            feed(x_res, by_chunk)

            for f0, nf in FFN_PARTS:
                with c.loop(pe, f"ffn_in{f0}", nf):
                    weights()
                    weights()
                    turn(left)
                pe.wait_ge(sem("tp_free"), c.value("tp_free"))
                if nf == 4:
                    with c.loop(pe, f"ffn_out{f0}", 4):
                        weights(kts=4 * nf, hi=ff_h, lo=ff_l)
                else:
                    with c.loop(pe, f"ffn_out{f0}", 2):
                        for b in range(2):
                            weights(kts=4 * nf, hi=ff_h, lo=ff_l)

            feed(merged2, by_chunk)
            for n in range(3):
                if n == 0:
                    pe.wait_ge(sem("wf_split"), 1)
                    for r in range(R):
                        k = 0
                        for kt in range(KT):
                            for x, w in ((x_hi, wf_hi), (x_hi, wf_lo), (x_lo, wf_hi)):
                                ins = mm(ps[:, AUX, r * 4:(r + 1) * 4], x[:, kt, r * P:(r + 1) * P],
                                         w[:, kt, :], start=k == 0, stop=k == 3 * KT - 1)
                                k += 1
                    ins.then_inc(sem("f_done"), 1)

                def turn_at_3(j):
                    if j == 3:
                        turn(nat_ready)

                def turn_raw(j):
                    if j == 3:
                        turn(left)

                def forget_at(j):
                    if n == 0 and j == 0:
                        pe.wait_ge(sem("logf_ready"), 1)
                        mm(ps[:, AUX, 0:4], upto[:, 0, 0:P], logf[:, 0, :], start=True, stop=True)
                        mm(ps[:, AUX, 4:8], upto[:, 0, P:S], logf[:, 0, :], start=True, stop=False)
                        mm(ps[:, AUX, 4:8], upto[:, 1, P:S], logf[:, 1, :], start=False, stop=True)\
                            .then_inc(sem("f_done"), 1)
                    if n == 0 and j % 2 == 1:
                        pe.wait_ge(sem("ck_in"), c.next("ck_in"))
                        for t in range(R):
                            ins = mm(ps[:, AUX, 0:S], ones[:, :], aux_a[:, t * S:(t + 1) * S],
                                     start=t == 0, stop=t == 1)
                        ins.then_inc(sem("f_done"), 1)
                    if j == 3:
                        turn(nat_ready if n < 2 else left)

                weights()
                weights(hook=turn_at_3 if n < 2 else turn_raw)
                weights(hook=forget_at)
                weights(hook=turn_raw)
                pe.wait_ge(sem("tp_free"), c.value("tp_free"))
                with c.loop(pe, f"branch{n}", 4) as i:
                    def soft(j):
                        if j == 0:
                            pe.wait_ge(sem("q_staged"), c.next("q_staged"))
                            scores([(q_st, lambda m: k2_t[:, ds(i, 1), 0:m])])
                        if j == 3:
                            turn_probs()
                        if j == 5:
                            outputs()

                    def stick(j):
                        if j == 0:
                            pe.wait_ge(sem("q_staged"), c.next("q_staged"))
                            pe.wait_ge(sem("s_read"), c.value("s_read"))
                            for t, (lo, hi) in enumerate(((0, S), (S, CW))):
                                ins = mm(ps[:, SC, lo:hi], q_st[:, t * P:(t + 1) * P],
                                         q2_t[:, ds(i, 1), t * P:S], start=True, stop=True)
                            ins.then_inc(sem("s_done"), 1)
                            c.next("s_read")
                        if j == 3:
                            pe.wait_ge(sem("p_ready"), c.next("p_ready"))
                            mm(ps[:, PT, 0:S], lower[:, :], aux_b[:, 0:S], start=True, stop=False)
                            mm(ps[:, PT, P:S], ones[:, :], aux_b[:, S:CW], start=False, stop=True)
                            mm(ps[:, PT, S:CW], lower[:, :], aux_b[:, S:CW], start=True, stop=True)\
                                .then_inc(sem("t_done"), 1)
                            c.next("pt_ready")
                        if j == 5:
                            outputs()
                    weights(hook=soft if n < 2 else stick)
                pe.wait_ge(sem("o_free"), c.value("o_free"))
                with c.loop(pe, f"up2_{n}", 2):
                    for b in range(2):
                        weights(kts=4, hi=y_h, lo=y_l)
            for r in range(R):
                pe.wait_ge(sem(f"tile_out{r}"), c.value(f"tile_out{r}"))
            pe.wait_ge(sem("summed"), c.at("summed2"))
            feed(merged2, lambda t: None)
            for b in range(4):
                weights()

        @block.scalar
        def _(act):
            c = Counts("act", per)

            def split():
                g = c.value("hi")
                if isinstance(g, int) and g >= N_GROUPS:
                    return
                slot = (c.base.get("hi", 0) + c.local.get("hi", 0)) % SLOTS
                act.wait_ge(sem(f"landed{slot}"), c.next(f"landed{slot}", 16))
                used = c.value("hi", SLOTS - 1)
                if some(used):
                    act.wait_ge(sem("w_used"), used)
                n = width(g)
                act.activation(w_hi[:, slot, :, 0:n], stage[:, slot, :, 0:n], ACT.Copy)\
                   .then_inc(sem("hi"), 1)
                c.next("hi")

            def weights(kts=KT, hook=None):
                for j in range(kts // GK):
                    split()
                    c.next("w_used")
                    if hook:
                        hook(j)

            def tile_done(r):
                if r == 0:
                    act.wait_ge(sem("tile0_done"), c.next("tile0_done"))
                else:
                    act.wait_ge(sem("w_used"), c.value("w_used"))

            def evac(dst, func=ACT.Copy, nat_free=True):
                for r in range(R):
                    tile_done(r)
                    if r == 0 and nat_free:
                        act.wait_ge(sem("tp_done"), c.value("tp_done"))
                    act.activation(dst(r), ps[:, ACC + r, :], func).then_inc(sem(f"tile_out{r}"), 1)
                    c.next(f"tile_out{r}")

            def to_nat(func=ACT.Copy):
                evac(lambda r: nat[:, r, :], func)

            def skip_block():
                c.next("tile0_done")
                for r in range(R):
                    c.next(f"tile_out{r}")

            def hi_part(dst, n):
                for t in range(n):
                    act.wait_ge(sem("tp_done"), c.next("tp_done"))
                    act.activation(dst(t), ps[:, TP + t % 2, :].rearrange("p (k s) -> p k s", k=2), ACT.Copy)\
                       .then_inc(sem("hi_t"), 1)

            def feed(dst, scale=None):
                if scale is None:
                    return hi_part(lambda t: dst[:, 2 * t:2 * t + 2, :], KT // 2)
                for t in range(KT // 2):
                    act.wait_ge(sem("tp_done"), c.next("tp_done"))
                    for k in range(2):
                        ins = act.activation(dst[:, 2 * t + k, :], ps[:, TP + t % 2, k * S:(k + 1) * S],
                                             ACT.Identity, scale=scale[:, 2 * t + k:2 * t + k + 1])
                    ins.then_inc(sem("hi_t"), 1)

            def root(x):
                act.wait_ge(sem("var"), c.next("var"))
                act.activation(x, x, ACT.Sqrt).then_inc(sem("root"), 1)

            def exps():
                act.wait_ge(sem("nmax"), c.next("nmax"))
                c.next("s_read")
                for t, (lo, hi) in enumerate(TILE_COLS):
                    ins = act.activation(logits[:, 0, lo:hi], logits[:, 0, lo:hi], ACT.Exp,
                                         bias=nmax[:, t:t + 1], accum_out=rsum[:, t:t + 1])
                ins.then_inc(sem("exp_done"), 1)

            def probs_out(used):
                act.wait_ge(sem("t_done"), c.next("t_done"))
                act.wait_ge(sem(used), c.value(used))
                act.activation(probs_t[:, 0:CW], ps[:, PT, 0:CW], ACT.Copy).then_inc(sem("pt_ready"), 1)

            def out_hi(dst):
                act.wait_ge(sem("o_done"), c.next("o_done"))
                act.activation(dst, ps[:, OT, 0:S], ACT.Copy).then_inc(sem("oh_done"), 1)

            for name in TOKENS["act"]:
                act.nop().then_inc(sem(name), 1)
            for _ in range(AHEAD):
                split()
            feed(x_hi)
            weights()
            skip_block()
            root(sd[:, 0:R])
            weights()
            for r in range(R):
                tile_done(r)
                act.activation(lat_nat[:, r, :], ps[:, ACC + r, 0:LAT], ACT.Copy).then_inc(sem(f"tile_out{r}"), 1)
                c.next(f"tile_out{r}")
            root(sd[:, 0:R])
            with c.loop(act, "q_idx", 2):
                weights()
                to_nat()
                c.next("tp_done", 2)
            c.next("tp_done", 2)
            with c.loop(act, "q_dsa", 2):
                weights()
                to_nat()
                c.next("tp_done", 2)
            with c.loop(act, "qk_m", 4):
                def index_head(j):
                    if j % 2:
                        act.wait_ge(sem("idx_done"), c.next("idx_done"))
                        act.wait_ge(sem("relu_used"), c.value("relu_used"))
                        act.activation(relu_s[:, :], ps[:, AUX, 0:CW], ACT.Relu).then_inc(sem("idx_read"), 1)
                        c.next("relu_used")
                weights(hook=index_head)
                to_nat()
                c.next("tp_done", 2)
            for b in range(2):
                weights()
                evac(lambda r: vm[:, r, b * NB:(b + 1) * NB])
            with c.loop(act, "dsa", 4) as i:
                def aux_out(dst, used):
                    act.wait_ge(sem("x_done"), c.next("x_done"))
                    act.wait_ge(sem(used), c.value(used))
                    act.activation(dst[:, :], ps[:, AUX, :], ACT.Copy).then_inc(sem("x_ready"), 1)

                def dsa(j):
                    if j in (0, 2):
                        aux_out(aux_a, "s_done")
                    elif j == 1:
                        c.next("s_done")
                        exps()
                    elif j == 3:
                        probs_out("x_done")
                    elif j == 4:
                        aux_out(aux_b, "o_done")
                        c.next("s_done")
                        exps()
                    elif j == 5:
                        out_hi(flat(oh[:, ds(i * 2, 1), :]))
                    elif j == 6:
                        probs_out("x_done")
                    elif j == 7:
                        aux_out(aux_b, "o_done")
                        out_hi(flat(oh[:, ds(i * 2 + 1, 1), :]))
                weights(hook=dsa)
                skip_block()

            def up(name, gate):
                with c.loop(act, name, 4) as i:
                    g = gate[:, :, ds(i * NB, NB)]
                    for r in range(R):
                        act.wait_ge(sem(f"tile_out{r}"), c.value(f"tile_out{r}"))
                    act.activation(g, g, ACT.Sigmoid).then_inc(sem("gate_ready"), 1)
                    weights(kts=8)
                    skip_block()
            up("up_a", gate_a)
            with c.loop(act, "moba", 4) as i:
                def moba(j):
                    if j in (0, 3):
                        if j == 3:
                            out_hi(flat(oh[:, ds(i * 2, 1), :]))
                        exps()
                    if j in (2, 5):
                        probs_out("o_done")
                    if j == 6:
                        out_hi(flat(oh[:, ds(i * 2 + 1, 1), :]))
                weights(hook=moba)
                skip_block()
            up("up_b", gate_b)
            feed(x_hi)
            with c.loop(act, "w_out", 4):
                weights()
                skip_block()
            feed(mem_hi)
            def ln_root(j):
                if j == 0:
                    root(sd[:, 0:R])
            weights(hook=ln_root)
            to_nat()
            c.next("tp_done", 2)
            weights()
            evac(lambda r: vmem[:, r, :])
            feed(x_hi)
            weights()
            to_nat()
            c.next("tp_done", 2)

            def mem_exps(h):
                act.wait_ge(sem("nmax"), c.next("nmax"))
                act.wait_ge(sem("t_done"), c.value("t_done"))
                for r in range(R):
                    ins = act.activation(logits[:, h % 2, r * S:(r + 1) * S],
                                         ps[:, SC + h % 2, r * S:(r + 1) * S], ACT.Exp, scale=SCALE,
                                         bias=nmax[:, r:r + 1], accum_out=rsum[:, r:r + 1])
                ins.then_inc(sem("s_read"), 1)
                c.next("s_read")

            mem_exps(0)
            for h in range(H_MEM):
                if h + 1 < H_MEM:
                    mem_exps(h + 1)
                act.wait_ge(sem("t_done"), c.next("t_done"))
                act.wait_ge(sem("o_done"), c.value("o_done"))
                act.activation(probs_t[:, :], ps[:, PT, :], ACT.Copy).then_inc(sem("pt_ready"), 1)
                out_hi(om_h[:, h, :])
            for b in range(4):
                weights(kts=4)
                skip_block()
            root(sd[:, 0:R])
            feed(x_hi)
            for f0, nf in FFN_PARTS:
                with c.loop(act, f"ffn_in{f0}", nf) as i:
                    weights()
                    evac(lambda r: silu_g[:, r, :], ACT.Silu, nat_free=False)
                    weights()
                    skip_block()
                    hi_part(lambda t: ff_h[:, ds(i * 4 + 2 * t, 2), :], 2)
                if nf == 4:
                    with c.loop(act, f"ffn_out{f0}", 4):
                        weights(kts=4 * nf)
                        skip_block()
                else:
                    with c.loop(act, f"ffn_out{f0}", 2):
                        for b in range(2):
                            weights(kts=4 * nf)
                            skip_block()
            root(sd[:, 0:R])
            pe_free = c.value("t_done")
            for n in range(4):
                act.wait_ge(sem("chunk3"), n + 1)
                if n == 0:
                    act.wait_ge(sem("t_done"), pe_free)
                for r in range(R):
                    ins = act.activation(logits[:, r, :], x_res[:, r, n * NB:(n + 1) * NB], ACT.Square,
                                         accum_out=ssq[:, r * 4 + n:r * 4 + n + 1])
                    ins.then_inc(sem("squares"), 1)
                    act.wait_ge(sem("squares"), c.next("squares"))
            root(sd[:, 0:R])
            act.wait_ge(sem("small2"), 64)
            act.activation(wf_hi[:, :, :], wf[:, :, :], ACT.Copy).then_inc(sem("wf_hi"), 1)
            feed(x_hi, scale=g_col)

            def log1p_exp(x, src, count):
                act.wait_ge(sem(count), c.next(count))
                act.activation(x, src, ACT.Abs).then_inc(sem("act_step"), 1)
                act.wait_ge(sem("act_step"), c.next("act_step"))
                act.activation(x, x, ACT.Exp, scale=-1.0).then_inc(sem("act_step"), 1)
                act.wait_ge(sem("act_step"), c.next("act_step"))
                act.activation(x, x, ACT.Ln, bias=1.0).then_inc(sem("ln_done"), 1)

            for n in range(3):
                def q_norm(j):
                    if n < 2 and j == 0:
                        root(sd[:, :])
                if n == 0:
                    log1p_exp(f_b[:, :, :], f_a[:, :, :], "az")
                weights()
                to_nat()
                c.next("tp_done", 2)
                weights(hook=q_norm)
                to_nat()
                c.next("tp_done", 2)
                weights(hook=q_norm)
                to_nat(ACT.Silu)
                c.next("tp_done", 2)
                weights()
                evac(lambda r: v2[:, r, :], nat_free=False)
                with c.loop(act, f"branch{n}", 4) as i:
                    def soft(j):
                        if j == 0:
                            exps()
                        if j == 3:
                            probs_out("o_done")

                    def stick(j):
                        if j == 0:
                            log1p_exp(aux_b[:, 0:CW], logits[:, 1, 0:CW], "s_read")
                        if j == 3:
                            c.next("t_done")
                            act.wait_ge(sem("nmax"), c.next("nmax"))
                            act.wait_ge(sem("o_done"), c.value("o_done"))
                            act.activation(probs_t[:, 0:CW], logits[:, 0, 0:CW], ACT.Exp)\
                               .then_inc(sem("pt_ready"), 1)

                    def both(j):
                        (soft if n < 2 else stick)(j)
                        if j == 5:
                            c.next("o_done")
                            act.wait_ge(sem("y_ready"), c.next("y_ready"))
                            act.activation(flat(y_h[:, ds(i, 1), :]), aux_a[:, 0:S], ACT.Copy)\
                               .then_inc(sem("oh_done"), 1)
                    weights(hook=both)
                    skip_block()
                with c.loop(act, f"up2_{n}", 2) as i:
                    for b in range(2):
                        g = gate2[:, :, ds((i * 2 + b) * NB, NB)]
                        for r in range(R):
                            act.wait_ge(sem(f"tile_out{r}"), c.value(f"tile_out{r}"))
                        act.activation(g, g, ACT.Sigmoid).then_inc(sem("gate_ready"), 1)
                        weights(kts=4)
                        skip_block()
            feed(x_hi)
            for b in range(4):
                weights()
                skip_block()

        @block.vector
        def _(dve):
            c = Counts("dve", per)

            def split():
                g = c.value("lo_done")
                if isinstance(g, int) and g >= N_GROUPS:
                    return
                slot = (c.base.get("lo_done", 0) + c.local.get("lo_done", 0)) % SLOTS
                dve.wait_ge(sem("hi"), c.next("hi"))
                n = width(g)
                dve.tensor_tensor(w_lo[:, slot, :, 0:n], stage[:, slot, :, 0:n],
                                  w_hi[:, slot, :, 0:n].bitcast(F32), ALU.subtract).then_inc(sem("lo_done"), 1)
                c.next("lo_done")

            def weights(kts=KT, hook=None):
                for j in range(kts // GK):
                    split()
                    c.next("w_used")
                    if hook:
                        hook(j)

            def tile_done(r):
                if r == 0:
                    dve.wait_ge(sem("tile0_done"), c.next("tile0_done"))
                else:
                    dve.wait_ge(sem("w_used"), c.value("w_used"))

            def skip_block():
                c.next("tile0_done")
                for r in range(R):
                    c.next(f"tile_out{r}")

            def heads_in(dst, scale=None):
                for t in range(2):
                    dve.wait_ge(sem("tp_done"), c.next("tp_done"))
                    src = ps[:, TP + t, :].rearrange("p (k s) -> p k s", k=2)
                    if scale is None:
                        ins = dve.tensor_copy(dst(t), src)
                    else:
                        ins = dve.tensor_scalar(dst(t), src, scale, None, ALU.mult)
                    ins.then_inc(sem("tp_free"), 1)
                    c.next("tp_free")

            def lo_part(hi, lo, n):
                for t in range(n):
                    dve.wait_ge(sem("hi_t"), c.next("hi_t"))
                    dve.tensor_tensor(lo(t), ps[:, TP + t % 2, :].rearrange("p (k s) -> p k s", k=2),
                                      hi(t).bitcast(F32), ALU.subtract).then_inc(sem("tp_free"), 1)
                    c.next("tp_done")
                    c.next("tp_free")

            def feed(hi, lo, scale=None):
                if scale is None:
                    return lo_part(lambda t: hi[:, 2 * t:2 * t + 2, :], lambda t: lo[:, 2 * t:2 * t + 2, :],
                                   KT // 2)
                for t in range(KT // 2):
                    dve.wait_ge(sem("hi_t"), c.next("hi_t"))
                    for k in range(2):
                        ins = dve.scalar_tensor_tensor(
                            out=lo[:, 2 * t + k, :], in0=ps[:, TP + t % 2, k * S:(k + 1) * S],
                            scalar=scale[:, 2 * t + k:2 * t + k + 1], in1=hi[:, 2 * t + k, :].bitcast(F32),
                            op0=ALU.mult, op1=ALU.subtract)
                    ins.then_inc(sem("tp_free"), 1)
                    c.next("tp_done")
                    c.next("tp_free")

            def inverse_root(x, n, mean, eps):
                dve.tensor_scalar(sd[:, 0:n], x, mean, eps, ALU.mult, ALU.add).then_inc(sem("var"), 1)
                dve.wait_ge(sem("root"), c.next("root"))
                dve.reciprocal(rstd[:, 0:n], sd[:, 0:n]).then_inc(sem("dve_step"), 1)
                dve.wait_ge(sem("dve_step"), c.next("dve_step"))

            def logits_in(bias, op=ALU.add):
                dve.wait_ge(sem("s_done"), c.next("s_done"))
                dve.wait_ge(sem("t_done"), c.value("t_done"))
                dve.scalar_tensor_tensor(out=logits[:, 0, 0:CW], in0=ps[:, SC, 0:CW], scalar=SCALE,
                                         in1=bias, op0=ALU.mult, op1=op).then_inc(sem("s_read"), 1)
                dve.wait_ge(sem("s_read"), c.next("s_read"))
                for t, (lo, hi) in enumerate(TILE_COLS):
                    ins = dve.tensor_reduce(nmax[:, t:t + 1], logits[:, 0, lo:hi], AX.X, ALU.max)
                ins.then_inc(sem("dve_step"), 1)
                dve.wait_ge(sem("dve_step"), c.next("dve_step"))
                dve.tensor_scalar(nmax[:, :], nmax[:, :], -1.0, None, ALU.mult).then_inc(sem("nmax"), 1)

            def normalise(tiles, x, ready=("exp_done",)):
                dve.wait_ge(sem(ready[0]), c.next(ready[0]))
                dve.reciprocal(rinv[:, :], rsum[:, :]).then_inc(sem("dve_step"), 1)
                dve.wait_ge(sem("dve_step"), c.next("dve_step"))
                for t, (lo, hi) in enumerate(tiles):
                    ins = dve.tensor_scalar(x[:, lo:hi], x[:, lo:hi], rinv[:, t:t + 1], None, ALU.mult)
                ins.then_inc(sem("p_ready"), 1)

            def softmax(bias, op=ALU.add):
                logits_in(bias, op)
                normalise(TILE_COLS, logits[:, 0, :])

            def out_lo(hi, lo):
                dve.wait_ge(sem("oh_done"), c.next("oh_done"))
                c.next("o_done")
                dve.tensor_tensor(lo, ps[:, OT, 0:S], hi.bitcast(F32), ALU.subtract).then_inc(sem("o_free"), 1)

            def gates_in(gate, vec, i):
                for r in range(R):
                    tile_done(r)
                    dve.tensor_tensor(gate[:, r, ds(i * NB, NB)], ps[:, ACC + r, :], vec[:, ds(i * NB, NB)],
                                      ALU.add).then_inc(sem(f"tile_out{r}"), 1)
                    c.next(f"tile_out{r}")

            def gated(gate, merged, i, add):
                dve.wait_ge(sem("gate_ready"), c.next("gate_ready"))
                cols = ds(i * NB, NB)
                for r in range(R):
                    tile_done(r)
                    dst = gate if add else merged
                    dve.tensor_tensor(dst[:, r, cols], ps[:, ACC + r, :], gate[:, r, cols], ALU.mult)\
                       .then_inc(sem(f"tile_out{r}"), 1)
                    c.next(f"tile_out{r}")
                if add:
                    for r in range(R):
                        dve.wait_ge(sem(f"tile_out{r}"), c.value(f"tile_out{r}"))
                        dve.tensor_tensor(merged[:, r, cols], merged[:, r, cols], gate[:, r, cols], ALU.add)\
                            .then_inc(sem("summed"), 1)
                        dve.wait_ge(sem("summed"), c.next("summed"))

            def residual(i, alpha, stat):
                cols = ds(i * NB, NB)
                for r in range(R):
                    tile_done(r)
                    x = x_res[:, r, cols]
                    dve.scalar_tensor_tensor(out=x, in0=x, scalar=alpha, in1=ps[:, ACC + r, :],
                                             op0=ALU.mult, op1=ALU.add).then_inc(sem(f"tile_out{r}"), 1)
                    dve.wait_ge(sem(f"tile_out{r}"), c.next(f"tile_out{r}"))
                    if stat:
                        dve.bn_stats(flat(stats[:, r, ds(i, 1), :]), x).then_inc(sem("dve_step"), 1)
                        dve.wait_ge(sem("dve_step"), c.next("dve_step"))

            def norm_root(vecs):
                for r in range(R):
                    dve.bn_aggr(mv[:, r, :], flat(stats[:, r, :, :])).then_inc(sem("dve_step"), 1)
                    dve.wait_ge(sem("dve_step"), c.next("dve_step"))
                dve.wait_ge(sem("vec"), vecs)
                inverse_root(mv[:, :, 1], R, 1.0, LN_EPS)

            def norm_chunk(n, name="chunk"):
                cols = slice(n * NB, (n + 1) * NB)
                for r in range(R):
                    x = x_res[:, r, cols]
                    dve.scalar_tensor_tensor(out=x, in0=x, scalar=mv[:, r, 0:1], in1=vec_a[:, cols],
                                             op0=ALU.subtract, op1=ALU.mult).then_inc(sem("dve_step"), 1)
                    dve.wait_ge(sem("dve_step"), c.next("dve_step"))
                for r in range(R):
                    x = x_res[:, r, cols]
                    ins = dve.scalar_tensor_tensor(out=x, in0=x, scalar=rstd[:, r:r + 1], in1=vec_b[:, cols],
                                                   op0=ALU.mult, op1=ALU.add)
                ins.then_inc(sem(name), 1)
                c.next(name)

            for name in TOKENS["dve"]:
                dve.nop().then_inc(sem(name), 1)
            for _ in range(AHEAD):
                split()
            feed(x_hi, x_lo)
            weights()
            for r in range(R):
                tile_done(r)
                dve.tensor_copy(kidx2[:, r, 0:IDX_D], ps[:, ACC + r, 0:IDX_D])
                dve.tensor_scalar(w_idx[:, r, :], ps[:, ACC + r, IDX_D:KIDX_W],
                                  IDX_D ** -0.5 * IDX_H ** -0.5, None, ALU.mult)\
                   .then_inc(sem(f"tile_out{r}"), 1)
                dve.wait_ge(sem(f"tile_out{r}"), c.next(f"tile_out{r}"))
                dve.bn_stats(stats[:, r, 0, :], kidx2[:, r, 0:IDX_D]).then_inc(sem("dve_step"), 1)
                dve.wait_ge(sem("dve_step"), c.next("dve_step"))
                dve.bn_aggr(mv[:, r, :], stats[:, r, 0, :]).then_inc(sem("dve_step"), 1)
                dve.wait_ge(sem("dve_step"), c.next("dve_step"))
            inverse_root(mv[:, :, 1], R, 1.0, LN_EPS)
            dve.wait_ge(sem("small"), 48)
            for r in range(R):
                x = kidx2[:, r, 0:IDX_D]
                dve.scalar_tensor_tensor(out=x, in0=x, scalar=mv[:, r, 0:1], in1=ik_g[:, :],
                                         op0=ALU.subtract, op1=ALU.mult).then_inc(sem("dve_step"), 1)
                dve.wait_ge(sem("dve_step"), c.next("dve_step"))
                dve.scalar_tensor_tensor(out=x, in0=x, scalar=rstd[:, r:r + 1], in1=ik_b[:, :],
                                         op0=ALU.mult, op1=ALU.add).then_inc(sem("dve_step"), 1)
                dve.wait_ge(sem("dve_step"), c.next("dve_step"))
                ins = dve.tensor_copy(kidx2[:, r, IDX_D:2 * IDX_D], x)
            ins.then_inc(sem("nat_ready"), 1)
            weights()
            c.next("tile0_done")
            for r in range(R):
                dve.wait_ge(sem(f"tile_out{r}"), c.next(f"tile_out{r}"))
                dve.tensor_tensor(aux_a[:, 0:LAT], lat_nat[:, r, :], lat_nat[:, r, :], ALU.mult)\
                    .then_inc(sem("dve_step"), 1)
                dve.wait_ge(sem("dve_step"), c.next("dve_step"))
                dve.tensor_reduce(ssq[:, r:r + 1], aux_a[:, 0:LAT], AX.X, ALU.add).then_inc(sem("dve_step"), 1)
                dve.wait_ge(sem("dve_step"), c.next("dve_step"))
            inverse_root(ssq[:, 0:R], R, 1.0 / LAT, LN_EPS)
            for r in range(R):
                ins = dve.scalar_tensor_tensor(out=lat_nat[:, r, :], in0=lat_nat[:, r, :],
                                               scalar=rstd[:, r:r + 1], in1=kv_g[:, :],
                                               op0=ALU.mult, op1=ALU.mult)
            ins.then_inc(sem("nat_ready"), 1)
            dve.wait_ge(sem("ext"), 32)
            with c.loop(dve, "q_idx", 2) as i:
                weights()
                skip_block()
                heads_in(lambda t: qi_t[:, ds(i * 4 + 2 * t, 2), :])
            c.mark("q_idx", "tp_free")
            dve.wait_ge(sem("tp_done"), c.next("tp_done"))
            dve.tensor_copy(kidx_t[:, :], ps[:, TP, 0:S]).then_inc(sem("tp_free"), 1)
            dve.wait_ge(sem("tp_done"), c.next("tp_done"))
            dve.tensor_copy(lat_t[:, :, :], ps[:, TP + 1, :].rearrange("p (k s) -> p k s", k=2))\
               .then_inc(sem("tp_free"), 1)
            c.next("tp_free", 2)
            with c.loop(dve, "q_dsa", 2) as i:
                weights()
                skip_block()
                heads_in(lambda t: qd_t[:, ds(i * 4 + 2 * t, 2), :])
            dve.wait_ge(sem("const"), 1)
            with c.loop(dve, "qk_m", 4) as i:
                def index_head(j):
                    if j % 2 == 0:
                        return
                    dve.wait_ge(sem("idx_read"), c.next("idx_read"))
                    for t, (lo, hi) in enumerate(TILE_COLS):
                        ins = dve.scalar_tensor_tensor(
                            out=score[:, lo:hi], in0=relu_s[:, lo:hi],
                            scalar=flat(w_idx[:, t:t + 1, ds(i * 4 + j // 2, 1)]),
                            in1=score[:, lo:hi], op0=ALU.mult, op1=ALU.add)
                    ins.then_inc(sem("relu_used"), 1)
                    dve.wait_ge(sem("relu_used"), c.next("relu_used"))
                weights(hook=index_head)
                skip_block()
                heads_in(lambda t: qkm_t[:, ds(i * 4 + 2 * t, 2), :])

            def take8(t, rounds):
                lo, hi = TILE_COLS[t]
                for _ in range(rounds):
                    dve.max(best8[:, :], score[:, lo:hi]).then_inc(sem("dve_step"), 1)
                    dve.wait_ge(sem("dve_step"), c.next("dve_step"))
                    dve.match_replace(out=score[:, lo:hi], in_to_replace=best8[:, :],
                                      in_values=score[:, lo:hi], imm_value=TAKEN).then_inc(sem("dve_step"), 1)
                    dve.wait_ge(sem("dve_step"), c.next("dve_step"))

            dve.tensor_tensor(score[:, :], score[:, :], causal[:, :], ALU.add).then_inc(sem("dve_step"), 1)
            dve.wait_ge(sem("dve_step"), c.next("dve_step"))
            for b in range(2):
                weights(hook=lambda j: take8(b, 1))
                skip_block()
            dve.tensor_scalar(score[:, :], score[:, :], TAKEN / 2, NEG, ALU.is_gt, ALU.mult)\
                .then_inc(sem("dve_step"), 1)
            dve.wait_ge(sem("dve_step"), c.next("dve_step"))
            dve.tensor_tensor(bias_d[:, :], bias_m[:, :], score[:, :], ALU.add).then_inc(sem("dve_step"), 1)
            dve.wait_ge(sem("dve_step"), c.next("dve_step"))

            dve.wait_ge(sem("vec"), 32)
            with c.loop(dve, "dsa", 4) as i:
                def dsa(j):
                    if j == 0:
                        dve.tensor_scalar(bias_d[:, :], bias_d[:, :], 0.5, None, ALU.mult).then_inc(sem("dve_step"), 1)
                        dve.wait_ge(sem("dve_step"), c.next("dve_step"))
                    if j in (1, 4):
                        softmax(bias_d[:, :])
                    if j in (3, 6):
                        c.next("t_done")
                    if j == 3:
                        dve.tensor_scalar(bias_d[:, :], bias_d[:, :], 0.5, None, ALU.mult).then_inc(sem("dve_step"), 1)
                        dve.wait_ge(sem("dve_step"), c.next("dve_step"))
                    if j == 5:
                        out_lo(flat(oh[:, ds(i * 2, 1), :]), flat(ol[:, ds(i * 2, 1), :]))
                    if j == 7:
                        gates_in(gate_a, vec_a, i)
                        out_lo(flat(oh[:, ds(i * 2 + 1, 1), :]), flat(ol[:, ds(i * 2 + 1, 1), :]))
                weights(hook=dsa)
            with c.loop(dve, "up_a", 4) as i:
                weights(kts=8)
                gated(gate_a, gate_a, i, False)
            c.mark("mobas", "s_done")
            c.per[("mark", "mobao")] = 1 + H_DSA
            with c.loop(dve, "moba", 4) as i:
                def moba(j):
                    if j in (0, 3):
                        if j == 3:
                            out_lo(flat(oh[:, ds(i * 2, 1), :]), flat(ol[:, ds(i * 2, 1), :]))
                        dve.tensor_scalar(bias_m[:, :], bias_m[:, :], 0.5, None, ALU.mult).then_inc(sem("dve_step"), 1)
                        dve.wait_ge(sem("dve_step"), c.next("dve_step"))
                        softmax(bias_m[:, :])
                    if j in (2, 5):
                        c.next("t_done")
                    if j == 6:
                        out_lo(flat(oh[:, ds(i * 2 + 1, 1), :]), flat(ol[:, ds(i * 2 + 1, 1), :]))
                    if j == 7:
                        gates_in(gate_b, vec_b, i)
                weights(hook=moba)
            with c.loop(dve, "up_b", 4) as i:
                weights(kts=8)
                gated(gate_b, gate_a, i, True)
            c.mark("summed1", "summed")
            c.mark("merged", "tile_out1")
            feed(x_hi, x_lo)
            c.mark("fed", "tp_free")
            dve.wait_ge(sem("x_res"), 16)
            with c.loop(dve, "w_out", 4) as i:
                weights()
                residual(i, ALPHA, True)
            feed(mem_hi, mem_lo)

            def norm_in(j):
                if j == 0:
                    norm_root(64)
                if 1 <= j <= 4:
                    norm_chunk(j - 1)
            weights(hook=norm_in)
            c.mark("normed1", "chunk")
            skip_block()
            heads_in(lambda t: kmem_t[:, 2 * t:2 * t + 2, :])
            weights()
            skip_block()
            feed(x_hi, x_lo)
            weights()
            skip_block()
            heads_in(lambda t: qmem_t[:, 2 * t:2 * t + 2, :])

            def mem_max(h):
                dve.wait_ge(sem("s_done"), c.next("s_done"))
                dve.wait_ge(sem("s_read"), c.value("s_read"))
                src = ps[:, SC + h % 2, :].rearrange("p (r k) -> p r k", r=R)
                dve.tensor_reduce(nmax[:, :], src, AX.X, ALU.max).then_inc(sem("dve_step"), 1)
                dve.wait_ge(sem("dve_step"), c.next("dve_step"))
                dve.tensor_scalar(nmax[:, :], nmax[:, :], -SCALE, None, ALU.mult).then_inc(sem("nmax"), 1)

            mem_max(0)
            for h in range(H_MEM):
                normalise(((0, S), (S, 2 * S)), logits[:, h % 2, :], ("s_read",))
                if h + 1 < H_MEM:
                    mem_max(h + 1)
                c.next("t_done")
                out_lo(om_h[:, h, :], om_l[:, h, :])
            for b in range(4):
                weights(kts=4)
                residual(b, ALPHA, True)
            norm_root(96)
            for n in range(4):
                norm_chunk(n)
            c.mark("normed2", "chunk")
            feed(x_hi, x_lo)
            for f0, nf in FFN_PARTS:
                with c.loop(dve, f"ffn_in{f0}", nf) as i:
                    weights()
                    c.next("tile0_done")
                    for r in range(R):
                        c.next(f"tile_out{r}")
                    weights()
                    for r in range(R):
                        tile_done(r)
                        dve.wait_ge(sem(f"tile_out{r}"), c.value(f"tile_out{r}"))
                        if r == 0:
                            dve.wait_ge(sem("tp_done"), c.value("tp_done"))
                        dve.tensor_tensor(nat[:, r, :], ps[:, ACC + r, :], silu_g[:, r, :], ALU.mult)\
                           .then_inc(sem(f"tile_out{r}"), 1)
                    for r in range(R):
                        c.next(f"tile_out{r}")
                    lo_part(lambda t: ff_h[:, ds(i * 4 + 2 * t, 2), :],
                            lambda t: ff_l[:, ds(i * 4 + 2 * t, 2), :], 2)
                alpha = ALPHA if f0 == 0 else 1.0
                stat = f0 == FFN_PARTS[-1][0]
                if nf == 4:
                    with c.loop(dve, f"ffn_out{f0}", 4) as i:
                        weights(kts=4 * nf)
                        residual(i, alpha, stat)
                else:
                    with c.loop(dve, f"ffn_out{f0}", 2) as i:
                        for b in range(2):
                            weights(kts=4 * nf)
                            residual(i * 2 + b, alpha, stat)
            norm_root(128)
            for n in range(4):
                norm_chunk(n, "chunk3")
            dve.wait_ge(sem("squares"), 8)
            dve.tensor_reduce(mv[:, :, 0], ssq[:, :].rearrange("p (r n) -> p r n", r=R), AX.X, ALU.add)\
                .then_inc(sem("dve_step"), 1)
            dve.wait_ge(sem("dve_step"), c.next("dve_step"))
            inverse_root(mv[:, :, 0], R, 1.0 / D, EPS)
            dve.wait_ge(sem("small2"), 64)
            for n in range(4):
                for r in range(R):
                    cols = slice(n * NB, (n + 1) * NB)
                    ins = dve.tensor_scalar(merged2[:, r, cols], x_res[:, r, cols], rstd[:, r:r + 1], None,
                                            ALU.mult)
                ins.then_inc(sem("chunk"), 1)
                c.next("chunk")
            dve.wait_ge(sem("wf_hi"), 1)
            dve.tensor_tensor(wf_lo[:, :, :], wf[:, :, :], wf_hi[:, :, :].bitcast(F32), ALU.subtract)\
               .then_inc(sem("wf_split"), 1)
            feed(x_hi, x_lo, scale=g_col)

            def head_norm(j):
                if n == 2 or j != 0:
                    return
                for r in range(R):
                    dve.wait_ge(sem(f"tile_out{r}"), c.value(f"tile_out{r}"))
                    dve.tensor_tensor(aux_b[:, :], nat[:, r, :], nat[:, r, :], ALU.mult).then_inc(sem("dve_step"), 1)
                    dve.wait_ge(sem("dve_step"), c.next("dve_step"))
                    dve.tensor_reduce(ssq[:, r * 4:(r + 1) * 4],
                                      aux_b[:, :].rearrange("p (h d) -> p h d", h=4), AX.X, ALU.add)\
                        .then_inc(sem("dve_step"), 1)
                    dve.wait_ge(sem("dve_step"), c.next("dve_step"))
                inverse_root(ssq[:, :], 2 * 4, 1.0 / HD, EPS)
                for r in range(R):
                    x = nat[:, r, :].rearrange("p (h d) -> p h d", h=4)
                    by = rstd[:, r * 4:(r + 1) * 4].unsqueeze(2).to_broadcast([P, 4, HD])
                    ins = dve.tensor_tensor(x, x, by, ALU.mult)
                ins.then_inc(sem("nat_ready"), 1)

            for n in range(3):
                if n == 0:
                    dve.wait_ge(sem("f_done"), c.next("f_done"))
                    for r in range(R):
                        ins = dve.tensor_tensor(f_a[:, r, :], ps[:, AUX, r * 4:(r + 1) * 4], bf_v[:, :], ALU.add)
                    ins.then_inc(sem("az"), 1)
                    dve.wait_ge(sem("ln_done"), c.next("ln_done"))
                    dve.scalar_tensor_tensor(out=logf[:, :, :], in0=f_a[:, :, :], scalar=0.0, in1=f_b[:, :, :],
                                             op0=ALU.min, op1=ALU.subtract).then_inc(sem("logf_ready"), 1)
                weights()
                skip_block()

                def k_hook(j):
                    head_norm(j)
                    if j == 3:
                        heads_in(lambda t: q2_t[:, 2 * t:2 * t + 2, :],
                                 qk_g[:, 2 * n:2 * n + 1] if n < 2 else None)
                weights(hook=k_hook)
                skip_block()

                def g_hook(j):
                    head_norm(j)
                    if n == 0:
                        h = j // 2
                        if j == 0:
                            dve.wait_ge(sem("f_done"), c.next("f_done"))
                            dve.tensor_copy(c_q[:, :, :],
                                            ps[:, AUX, 0:8].rearrange("p (r h) -> p r h", r=R))\
                                .then_inc(sem("dve_step"), 1)
                            dve.wait_ge(sem("dve_step"), c.next("dve_step"))
                        if j % 2 == 0:
                            for t in range(R):
                                ins = dve.tensor_scalar(aux_a[:, t * S:(t + 1) * S], upto[:, t, :],
                                                        logf[:, t, h:h + 1], None, ALU.mult)
                            ins.then_inc(sem("ck_in"), 1)
                        else:
                            dve.wait_ge(sem("f_done"), c.next("f_done"))
                            for t, (lo, hi) in enumerate(TILE_COLS):
                                ins = dve.scalar_tensor_tensor(
                                    out=bias4[:, h, lo:hi], in0=ps[:, AUX, 0:hi - lo],
                                    scalar=c_q[:, t, h:h + 1], in1=causal[:, lo:hi],
                                    op0=ALU.subtract, op1=ALU.subtract)
                            ins.then_inc(sem("dve_step"), 1)
                            dve.wait_ge(sem("dve_step"), c.next("dve_step"))
                    if j == 3:
                        heads_in(lambda t: k2_t[:, 2 * t:2 * t + 2, :],
                                 qk_g[:, 2 * n + 1:2 * n + 2] if n < 2 else None)
                weights(hook=g_hook)
                skip_block()

                def v_hook(j):
                    if j == 3:
                        heads_in(lambda t: s2_t[:, 2 * t:2 * t + 2, :])
                    if n == 1 and j >= 4:
                        h = j - 4
                        if h == 0:
                            dve.wait_ge(sem("rel"), 16 * 8)
                            dve.wait_ge(sem("t_done"), c.value("t_done"))
                        for lo, hi in TILE_COLS:
                            ins = dve.tensor_copy(logits[:, 0, lo:hi], bias4[:, h, lo:hi][:, ::-1])
                        ins.then_inc(sem("dve_step"), 1)
                        dve.wait_ge(sem("dve_step"), c.next("dve_step"))
                        dve.tensor_copy(bias4[:, h, :], logits[:, 0, 0:CW]).then_inc(sem("dve_step"), 1)
                        dve.wait_ge(sem("dve_step"), c.next("dve_step"))
                        for _, hi in TILE_COLS:
                            ins = dve.memset(bias4[0:CHUNK, h, hi - CHUNK:hi], NEG)
                        ins.then_inc(sem("dve_step"), 1)
                        dve.wait_ge(sem("dve_step"), c.next("dve_step"))
                weights(hook=v_hook)
                skip_block()
                c.mark(f"q2_{n}", "tp_free")
                c.mark(f"v2_{n}", "tile_out1")
                c.mark(f"branch{n}s", "s_done")
                c.per[("mark", f"branch{n}o")] = 1 + c.value("oh_done")
                if n == 1:
                    c.mark("gates2_in", "tile_out1")
                dve.wait_ge(sem("vec"), 144 + 16 * n)
                with c.loop(dve, f"branch{n}", 4) as i:
                    def soft(j):
                        if j == 0:
                            softmax(flat(bias4[:, ds(i, 1), :]), ALU.subtract if n == 0 else ALU.add)
                        if j == 3:
                            c.next("t_done")

                    def stick(j):
                        if j == 0:
                            dve.wait_ge(sem("s_done"), c.next("s_done"))
                            dve.wait_ge(sem("t_done"), c.value("t_done"))
                            dve.tensor_scalar(logits[:, 1, 0:CW], ps[:, SC, 0:CW], SCALE, None, ALU.mult)\
                                .then_inc(sem("s_read"), 1)
                            dve.wait_ge(sem("s_read"), c.next("s_read"))
                            dve.wait_ge(sem("ln_done"), c.next("ln_done"))
                            dve.scalar_tensor_tensor(out=aux_b[:, 0:CW], in0=logits[:, 1, 0:CW], scalar=0.0,
                                                     in1=aux_b[:, 0:CW], op0=ALU.max, op1=ALU.add)\
                                .then_inc(sem("dve_step"), 1)
                            dve.wait_ge(sem("dve_step"), c.next("dve_step"))
                            dve.tensor_tensor(aux_b[:, 0:CW], aux_b[:, 0:CW], strict_t[:, :], ALU.add)\
                                .then_inc(sem("dve_step"), 1)
                            dve.wait_ge(sem("dve_step"), c.next("dve_step"))
                            dve.tensor_scalar(aux_b[:, 0:CW], aux_b[:, 0:CW], 0.0, None, ALU.max)\
                                .then_inc(sem("p_ready"), 1)
                            dve.wait_ge(sem("p_ready"), c.next("p_ready"))
                            dve.tensor_tensor(logits[:, 1, 0:CW], logits[:, 1, 0:CW], strict_t[:, :],
                                              ALU.add).then_inc(sem("dve_step"), 1)
                            dve.wait_ge(sem("dve_step"), c.next("dve_step"))
                        if j == 3:
                            dve.wait_ge(sem("t_done"), c.next("t_done"))
                            dve.tensor_tensor(logits[:, 0, 0:CW], logits[:, 1, 0:CW], ps[:, PT, 0:CW],
                                              ALU.subtract).then_inc(sem("nmax"), 1)
                            c.next("pt_ready")

                    def both(j):
                        (soft if n < 2 else stick)(j)
                        if j == 5:
                            dve.wait_ge(sem("o_done"), c.next("o_done"))
                            dve.tensor_tensor(aux_a[:, 0:S], ps[:, OT, 0:S], flat(s2_t[:, ds(i, 1), :]),
                                              ALU.mult).then_inc(sem("y_ready"), 1)
                            dve.wait_ge(sem("y_ready"), c.next("y_ready"))
                            dve.wait_ge(sem("oh_done"), c.next("oh_done"))
                            dve.tensor_tensor(flat(y_l[:, ds(i, 1), :]), aux_a[:, 0:S],
                                              flat(y_h[:, ds(i, 1), :]).bitcast(F32), ALU.subtract)\
                               .then_inc(sem("o_free"), 1)
                        if j == 7:
                            gates_in(gate2, vec_a, i)
                    weights(hook=both)
                c.mark(f"gates2_{n}", "tile_out1")
                if n == 0:
                    c.mark("forget", "s_read")
                with c.loop(dve, f"up2_{n}", 2) as i:
                    for b in range(2):
                        weights(kts=4)
                        gated(gate2, merged2, i * 2 + b, n > 0)
            c.mark("summed2", "summed")
            feed(x_hi, x_lo)
            for b in range(4):
                weights()
                residual(b, 1.0, False)
                c.mark(f"final{b}", "tile_out1")


_INS = {
    "x": ("x", (S, D)), "mem": ("mem", (S, D)), "w_in": ("w_in", (D, C_GB + D)), "b_gate": ("b_gate", (2, D)),
    "kv_norm_g": ("kv_norm_g", (LAT,)), "idx_k_norm_g": ("idx_k_norm_g", (IDX_D,)),
    "idx_k_norm_b": ("idx_k_norm_b", (IDX_D,)), "w_uk": ("w_uk", (H_DSA * HD, LAT)),
    "w_uv": ("w_uv", (H_DSA * LAT, HD)), "w_o_dsa": ("w_o_dsa", (H_DSA * HD, D)),
    "w_o_moba": ("w_o_moba", (H_MOBA * HD, D)), "w_out": ("w_out", (D, D)),
    "w_q_mem": ("w_q_mem", (D, H_MEM * HD)), "w_kv_mem": ("w_kv_mem", (D, 2 * H_MEM * HD)),
    "w_o_mem": ("w_o_mem", (H_MEM * HD, D)), "w_ffn_in": ("w_ffn_in", (D, 2 * D_FF)),
    "w_ffn_out": ("w_ffn_out", (D_FF, D)), "ln_g": ("ln_g", (3, D)), "ln_b": ("ln_b", (3, D)),
    "norm_g": ("norm_g_2", (D,)), "w_in_2": ("w_in_2", (D, C_G2 + 3 * D)), "b_f": ("b_f_2", (H_B2,)),
    "b_gate_2": ("b_gate_2", (1, 3 * D)), "qk_norm_g": ("qk_norm_g_2", (4, HD)),
    "rel_bias": ("rel_bias_2", (H_B2, 2 * MAX_REL + 1)), "w_up_2": ("w_up_2", (3 * BR_W, D)),
    "w_out_2": ("w_out_2", (D, D)),
}


def lay_out(nc, shapes, per):
    a = {k: nc.dram_tensor("in_" + k, list(s), F32, kind="ExternalInput").ap() for k, s in shapes.items()}
    out = nc.dram_tensor("out", [S, D], F32, kind="ExternalOutput").ap()
    two_blocks(nc, a, out, per)


def kernel(**inputs):
    import numpy as np
    import concourse.bacc as bacc
    from concourse.bass_utils import run_bass_kernel_spmd

    shapes = {k: s for k, (_, s) in _INS.items()}
    per = {"counting": 1}
    lay_out(bacc.Bacc("TRN2", target_bir_lowering=False, num_devices=1), shapes, per)
    del per["counting"]
    nc = bacc.Bacc("TRN2", target_bir_lowering=False, num_devices=1)
    lay_out(nc, shapes, per)
    arrays = {"in_" + k: np.ascontiguousarray(inputs[name]).reshape(s) for k, (name, s) in _INS.items()}
    r = run_bass_kernel_spmd(nc, [arrays], core_ids=[0])
    return r.results[0]["out"].reshape(1, S, D)
```

```python
from contextlib import ExitStack, contextmanager

import concourse.bass as bass
from concourse import mybir

F32 = mybir.dt.float32
F32R = mybir.dt.float32r
ACT = mybir.ActivationFunctionType
ALU = mybir.AluOpType
AX = mybir.AxisListType
ds = bass.ds

P = 128
S = 256
R = S // P
D = 2048
KT = D // P
HD = 128
NB = 512
GK = 2
SLOTS = 4
AHEAD = 2
H_DSA, H_MOBA, H_MEM, H_B2 = 8, 8, 4, 4
LAT, IDX_H, IDX_D = 256, 16, 64
TOPK = S // 4
D_FF = -(-8 * D // (3 * 256)) * 256
BR_W = H_B2 * HD
MAX_REL = 128
CHUNK = 64
ALPHA = 2.0 ** 0.25
SCALE = HD ** -0.5
LN_EPS = 1e-5
EPS = 1e-6
NEG = -1e30
TAKEN = -3e38
CW = P + S
TILE_COLS = ((0, P), (P, CW))

C_QDSA = 0
C_LAT = C_QDSA + H_DSA * HD
C_QIDX = C_LAT + LAT
C_KIDX = C_QIDX + IDX_H * IDX_D
C_QM = C_KIDX + IDX_D + IDX_H
C_VM = C_QM + 2 * H_MOBA * HD
C_GA = C_VM + H_MOBA * HD
C_GB = C_GA + D
C_F = 3 * 4 * BR_W
C_G2 = C_F + H_B2
KIDX_W = IDX_D + IDX_H
FIRST_W = LAT + KIDX_W
FFN_PARTS = ((0, 4), (4, 4), (8, 3))
G_UV = (1 + 2 + 2 + 4 + 2) * KT // GK
N_GROUPS = (
    G_UV + H_DSA * HD // NB + 2 * 4 * (KT // GK + 8 // GK) + 4 * KT // GK
    + 2 * KT // GK + KT // GK + 4 * 4 // GK + 2 * (D_FF // NB) * KT // GK + 4 * D_FF // P // GK
    + 3 * (4 * KT // GK + 4 * KT // GK + 4 * 4 // GK) + 4 * KT // GK
)


TOKENS = {
    "pe": ("s_done", "t_done", "x_done", "o_done"),
    "act": ("x_ready", "pt_ready", "idx_read"),
    "dve": ("s_read", "o_free", "relu_used"),
}


class Counts:

    def __init__(self, engine, per):
        self.engine, self.per, self.local, self.loop_at = engine, per, {}, None
        self.base = {name: 1 for names in TOKENS.values() for name in names}

    def value(self, name, back=0):
        fixed = self.base.get(name, 0) + self.local.get(name, 0) - back
        if self.loop_at is None:
            return fixed
        i, key = self.loop_at
        step = self.per.get((key, name), 0)
        assert fixed > 0 or step == 0 or self.per.get("counting"), (key, name, fixed)
        return fixed + i * step if step else fixed

    def next(self, name, n=1):
        self.local[name] = self.local.get(name, 0) + n
        return self.value(name)

    def mark(self, mark, name):
        self.per[("mark", mark)] = self.value(name)

    def at(self, mark):
        return self.per.get(("mark", mark), 1)

    @contextmanager
    def loop(self, eng, name, n):
        for k, v in self.local.items():
            self.base[k] = self.base.get(k, 0) + v
        self.local = {}
        key = (self.engine, name)
        with eng.Fori(0, n) as i:
            self.loop_at = (i, key)
            yield i
        self.loop_at = None
        for k, v in self.local.items():
            if self.per.get("counting"):
                self.per[(key, k)] = v
            assert self.per[(key, k)] == v
            self.base[k] = self.base.get(k, 0) + n * v
        self.local = {}


def some(value):
    return not isinstance(value, int) or value > 0


def two_blocks(nc, a, out, per):
    ctx = ExitStack()
    with ctx:
        def sb(name, shape, dt=F32):
            return ctx.enter_context(nc.sbuf_tensor("b_" + name, shape, dt))

        sems = {}

        def sem(name):
            if name not in sems:
                sems[name] = ctx.enter_context(nc.semaphore("s_" + name))
            return sems[name]

        stage = sb("stage", [P, SLOTS, GK, NB])
        w_hi = sb("w_hi", [P, SLOTS, GK, NB], F32R)
        w_lo = sb("w_lo", [P, SLOTS, GK, NB], F32R)
        x_hi = sb("x_hi", [P, KT, S], F32R)
        x_lo = sb("x_lo", [P, KT, S], F32R)
        vec_a = sb("vec_a", [P, D])
        vec_b = sb("vec_b", [P, D])
        ident = sb("ident", [P, P])
        ones = sb("ones", [P, P])
        causal = sb("causal", [P, CW])
        strict_t = sb("strict_t", [P, CW])
        lower = sb("lower", [P, P])
        nat = sb("nat", [P, R, NB])
        logits = sb("logits", [P, 2, NB])
        probs_t = sb("probs_t", [P, NB])
        aux_a = sb("aux_a", [P, NB])
        aux_b = sb("aux_b", [P, NB])
        q_st = sb("q_st", [P, S])
        v_st = sb("v_st", [P, R, HD])
        best8 = sb("best8", [P, 8])
        qk_g = sb("qk_g", [P, 4])
        bf_v = sb("bf_v", [P, H_B2])
        logf = sb("logf", [P, R, H_B2])
        f_a = sb("f_a", [P, R, H_B2])
        f_b = sb("f_b", [P, R, H_B2])
        c_q = sb("c_q", [P, R, H_B2])
        stats = sb("stats", [P, R, 4, 6])
        mv = sb("mv", [P, R, 2])
        sd = sb("sd", [P, R * 4])
        rstd = sb("rstd", [P, R * 4])
        ssq = sb("ssq", [P, R * 4])
        rms = sb("rms", [P, R])
        nmax = sb("nmax", [P, R])
        mem_max = sb("mem_max", [P, H_MEM, R])
        mem_sum = sb("mem_sum", [P, H_MEM, R])
        mem_inv = sb("mem_inv", [P, H_MEM, R])
        rsum = sb("rsum", [P, R])
        rinv = sb("rinv", [P, R])

        def shared(*shapes):
            with ExitStack() as own:
                return [own.enter_context(nc.sbuf_tensor("b_" + n, s, t)) for n, s, t in shapes]

        (qi_st, relu_s, score, lat_nat, lat_t, kidx2, kidx_t, w_uk_st, bias_d, bias_m, w_idx, kv_g,
         ik_g, ik_b) = shared(
            ("qi_st", [P, 2, S], F32),
            ("relu_s", [P, CW], F32),
            ("score", [P, CW], F32),
            ("lat_nat", [P, R, LAT], F32),
            ("lat_t", [P, 2, S], F32),
            ("kidx2", [P, R, 2 * IDX_D], F32),
            ("kidx_t", [P, S], F32),
            ("w_uk_st", [P, LAT], F32),
            ("bias_d", [P, CW], F32),
            ("bias_m", [P, CW], F32),
            ("w_idx", [P, R, IDX_H], F32),
            ("kv_g", [P, LAT], F32),
            ("ik_g", [P, IDX_D], F32),
            ("ik_b", [P, IDX_D], F32),
        )
        bias4 = sb("bias4", [P, H_B2, CW], F32)
        silu_g = sb("silu_g", [P, R, NB], F32)
        upto = sb("upto", [P, R, S], F32)
        wf = sb("wf", [P, KT, H_B2], F32)
        wf2 = sb("wf2", [P, KT, 2 * H_B2], F32R)
        f_t = sb("f_t", [2 * H_B2, S], F32)
        g_col = sb("g_col", [P, KT], F32)
        sb("pad_small", [P, 1024])
        (qkm_t, vm, qi_t, qd_t, oh, ol, gate_a) = shared(
            ("qkm_t", [P, 2 * H_MOBA, S], F32), ("vm", [P, R, H_MOBA * HD], F32),
            ("qi_t", [P, IDX_H // 2, S], F32), ("qd_t", [P, H_DSA, S], F32),
            ("oh", [P, H_DSA, S], F32R), ("ol", [P, H_DSA, S], F32R), ("gate_a", [P, R, D], F32))
        (_, _, v_dsa) = shared(
            ("pad1", [P, 2 * H_MOBA, S], F32), ("pad2", [P, R, H_MOBA * HD], F32),
            ("v_dsa", [P, R, H_DSA * HD], F32))
        (_, gate_b) = shared(("pad", [P, 3 * 8 * S], F32), ("gate_b", [P, R, D], F32))
        x_res = sb("x_res", [P, R, D])
        (mem_nat, mem_hi, mem_lo, kmem_t, vmem) = shared(
            ("mem_nat", [P, R, D], F32), ("mem_hi", [P, KT, S], F32R), ("mem_lo", [P, KT, S], F32R),
            ("kmem_t", [P, H_MEM, S], F32), ("vmem", [P, R, H_MEM * HD], F32))
        (qmem_t, om_h, om_l) = shared(
            ("qmem_t", [P, H_MEM, S], F32), ("om_h", [P, H_MEM, S], F32R), ("om_l", [P, H_MEM, S], F32R))
        (ff_h, ff_l) = shared(("ff_h", [P, 4 * 4, S], F32R), ("ff_l", [P, 4 * 4, S], F32R))
        (q2_t, k2_t, v2, s2_t, y_h, y_l, gate2, merged2) = shared(
            ("q2_t", [P, H_B2, S], F32), ("k2_t", [P, H_B2, S], F32), ("v2", [P, R, BR_W], F32),
            ("s2_t", [P, H_B2, S], F32), ("y_h", [P, H_B2, S], F32R), ("y_l", [P, H_B2, S], F32R),
            ("gate2", [P, R, D], F32), ("merged2", [P, R, D], F32))
        lat_hi, lat_lo = oh[:, 0:2, :], ol[:, 0:2, :]
        x_in = gate_a
        ps = ctx.enter_context(nc.psum_tensor("b_ps", [P, 8, NB], F32))
        ACC, TP, SC, AUX, PT, OT = 0, 2, 4, 5, 6, 7
        MEM_SC, MEM_PT = (ACC, ACC + 1, SC, AUX), (PT, TP, TP + 1, PT)
        mem_exp = (logits[:, 0, :], logits[:, 1, :], nat[:, 0, :], nat[:, 1, :])
        mem_pt = (probs_t, aux_a, probs_t, aux_a)
        mem_out = [ps[:, bank, 0:S] for bank in (OT, ACC, OT, ACC)]
        ext = nc.dram_tensor("rel_ext", [H_B2, 2 * S - 1], F32).ap()
        block = ctx.enter_context(nc.Block())

        def flat(x):
            return x.rearrange("p a n -> p (a n)")

        def width(g):
            return NB if not isinstance(g, int) or g >= KT // GK else FIRST_W

        @block.sync
        def _(sp):
            c = Counts("sp", per)

            def group(w, row, col, n=NB):
                slot = c.local.get("g", 0) + (c.base.get("g", 0))
                slot %= SLOTS
                back = c.value("g", SLOTS - 1)
                if some(back):
                    sp.wait_ge(sem("lo_done"), back)
                for at, width_, to in ((col, n, 0),) if n == NB else ((C_LAT, LAT, 0), (C_KIDX, KIDX_W, LAT)):
                    src = w[row:row + GK * P, ds(at, width_)].rearrange("(t p) n -> p t n", p=P)
                    sp.dma_start(stage[:, slot, :, to:to + width_], src).then_inc(sem(f"landed{slot}"), 16)
                c.next("g")

            def blockw(w, row, col, kts=KT, n=NB):
                for j in range(kts // GK):
                    group(w, row + j * GK * P, col, n)

            def blocks(name, w, row, col, count, kts=KT):
                with c.loop(sp, name, count) as i:
                    blockw(w, row, col + i * NB, kts)

            for n in range(D // NB):
                cols = slice(n * NB, (n + 1) * NB)
                sp.dma_start(x_in[:, :, cols], a["x"][:, cols].rearrange("(r p) n -> p r n", p=P))\
                  .then_inc(sem(f"x_in{n}"), 16)
                for j in range(2):
                    group(a["w_in"], (n * 2 + j) * GK * P, C_LAT, FIRST_W)
            blocks("q_idx", a["w_in"], 0, C_QIDX, 2)
            blocks("q_dsa", a["w_in"], 0, C_QDSA, 2)
            blocks("qk_m", a["w_in"], 0, C_QM, 4)
            for b in range(2):
                blockw(a["w_in"], 0, C_VM + b * NB)
            for b in range(H_DSA * HD // NB):
                slot = c.value("g") % SLOTS
                sp.wait_ge(sem("lo_done"), c.value("g", SLOTS - 1))
                src = a["w_uv"][b * 4 * LAT:(b + 1) * 4 * LAT, :].rearrange("(h t p) d -> t p h d", p=P, t=GK)
                for t in range(GK):
                    sp.dma_start(stage[:, slot, t, :].rearrange("p (h d) -> p h d", h=4), src[t])\
                      .then_inc(sem(f"landed{slot}"), 16)
                c.next("g")
            for gcol, wo in ((C_GA, a["w_o_dsa"]), (C_GB, a["w_o_moba"])):
                blocks(f"gate{gcol}", a["w_in"], 0, gcol, 4)
                blocks(f"up{gcol}", wo, 0, 0, 4, 8)
            blocks("w_out", a["w_out"], 0, 0, 4)
            for b in range(2):
                blockw(a["w_kv_mem"], 0, b * NB)
            blockw(a["w_q_mem"], 0, 0)
            for b in range(4):
                blockw(a["w_o_mem"], 0, b * NB, 4)
            for f0, nf in FFN_PARTS:
                with c.loop(sp, f"ffn_in{f0}", nf) as i:
                    blockw(a["w_ffn_in"], 0, (i + f0) * NB)
                    blockw(a["w_ffn_in"], 0, (i + f0) * NB + D_FF)
                if nf == 4:
                    blocks(f"ffn_out{f0}", a["w_ffn_out"], f0 * NB, 0, 4, 4 * nf)
                else:
                    with c.loop(sp, f"ffn_out{f0}", 2) as i:
                        for b in range(2):
                            blockw(a["w_ffn_out"], f0 * NB, (i * 2 + b) * NB, 4 * nf)
            for n in range(3):
                for b in range(4):
                    blockw(a["w_in_2"], 0, (4 * n + (0, 1, 3, 2)[b]) * BR_W)
                blocks(f"gate2_{n}", a["w_in_2"], 0, C_G2 + n * D, 4)
                with c.loop(sp, f"up2_{n}", 2) as i:
                    for b in range(2):
                        blockw(a["w_up_2"], n * BR_W, (i * 2 + b) * NB, 4)
            for b in range(4):
                blockw(a["w_out_2"], 0, b * NB)
            assert c.value("g") == N_GROUPS, (c.value("g"), N_GROUPS)
            for b in range(4):
                sp.wait_ge(sem("tile_out1"), c.at(f"final{b}"))
                sp.dma_start(out[:, b * NB:(b + 1) * NB].rearrange("(r p) n -> p r n", p=P),
                             x_res[:, :, b * NB:(b + 1) * NB]).then_inc(sem("out"), 16)
            sp.wait_ge(sem("out"), 16 * 4)

        @block.gpsimd
        def _(pool):
            c = Counts("pool", per)

            def load(dst, src, name, **how):
                pool.dma_start(dst, src, **how).then_inc(sem(name), 16)

            def rows(v):
                return v.partition_broadcast(P)

            pool.memset(ident[:, :], 0.0).then_inc(sem("pool_step"), 1)
            pool.wait_ge(sem("pool_step"), c.next("pool_step"))
            pool.affine_select(out=ident[:, :], in_=ident[:, :], compare_op=ALU.not_equal, fill=1.0,
                               base=0, pattern=[[-1, P]], channel_multiplier=1).then_inc(sem("ident"), 1)
            load(kv_g[:, :], rows(a["kv_norm_g"]), "small")
            load(ik_g[:, :], rows(a["idx_k_norm_g"]), "small")
            load(ik_b[:, :], rows(a["idx_k_norm_b"]), "small")
            pool.memset(ones[:, :], 1.0).then_inc(sem("pool_step"), 1)
            pool.wait_ge(sem("pool_step"), c.next("pool_step"))
            pool.memset(causal[:, :], 0.0).then_inc(sem("pool_step"), 1)
            pool.wait_ge(sem("pool_step"), c.next("pool_step"))
            pool.memset(strict_t[:, :], 0.0).then_inc(sem("pool_step"), 1)
            pool.wait_ge(sem("pool_step"), c.next("pool_step"))
            pool.memset(lower[:, :], 1.0).then_inc(sem("pool_step"), 1)
            pool.wait_ge(sem("pool_step"), c.next("pool_step"))
            pool.iota(bias_m[:, 0:P], pattern=[[1, P]], base=0, channel_multiplier=-1,
                      allow_small_or_imprecise_dtypes=True).then_inc(sem("pool_step"), 1)
            pool.wait_ge(sem("pool_step"), c.next("pool_step"))
            pool.iota(bias_m[:, P:CW], pattern=[[1, S]], base=-P, channel_multiplier=-1,
                      allow_small_or_imprecise_dtypes=True).then_inc(sem("pool_step"), 1)
            pool.wait_ge(sem("pool_step"), c.next("pool_step"))
            for t, (lo, hi) in enumerate(TILE_COLS):
                pool.affine_select(out=causal[:, lo:hi], in_=causal[:, lo:hi], compare_op=ALU.is_ge,
                                   fill=NEG, base=t * P, pattern=[[-1, hi - lo]], channel_multiplier=1)\
                    .then_inc(sem("pool_step"), 1)
                pool.wait_ge(sem("pool_step"), c.next("pool_step"))
                pool.affine_select(out=bias_m[:, lo:hi], in_=bias_m[:, lo:hi], compare_op=ALU.is_ge,
                                   fill=NEG, base=t * P, pattern=[[-1, hi - lo]], channel_multiplier=1)\
                    .then_inc(sem("pool_step"), 1)
                pool.wait_ge(sem("pool_step"), c.next("pool_step"))
            for t, (lo, hi) in enumerate(((0, S), (S, CW))):
                pool.affine_select(out=strict_t[:, lo:hi], in_=strict_t[:, lo:hi], compare_op=ALU.is_gt,
                                   fill=NEG, base=0, pattern=[[1, hi - lo]], channel_multiplier=-1)\
                    .then_inc(sem("pool_step"), 1)
                pool.wait_ge(sem("pool_step"), c.next("pool_step"))
            pool.affine_select(out=lower[:, :], in_=lower[:, :], compare_op=ALU.is_ge, fill=0.0,
                               base=0, pattern=[[-1, P]], channel_multiplier=1).then_inc(sem("pool_step"), 1)
            pool.wait_ge(sem("pool_step"), c.next("pool_step"))
            pool.memset(score[:, :], 0.0).then_inc(sem("const"), 1)

            side = S - 1 - MAX_REL
            row = gate_b[0:H_B2, 0, 0:2 * S - 1]
            load(row[:, side:side + 2 * MAX_REL + 1], a["rel_bias"], "ext")
            pool.wait_ge(sem("ext"), 16)
            for edge, at in ((row[:, 0:side], side), (row[:, side + 2 * MAX_REL + 1:], side + 2 * MAX_REL)):
                pool.tensor_copy(edge, row[:, at:at + 1].to_broadcast([H_B2, side])).then_inc(sem("pool_step"), 1)
                pool.wait_ge(sem("pool_step"), c.next("pool_step"))
            load(ext, row, "ext")

            pool.wait_ge(sem("tp_free"), c.at("q_idx"))
            pool.tensor_copy(qi_st[:, :, :], qi_t[:, 0:2, :]).then_inc(sem("qi_staged"), 1)
            load(vec_a[:, :], rows(a["b_gate"][0, :]), "vec")
            load(vec_b[:, :], rows(a["b_gate"][1, :]), "vec")
            load(w_uk_st[:, :], a["w_uk"][0:HD, :], "uk")
            with c.loop(pool, "qk_m", 3) as i:
                pool.wait_ge(sem("idx_done"), c.next("idx_done", 4))
                pool.tensor_copy(qi_st[:, :, :], qi_t[:, ds(i * 2 + 2, 2), :]).then_inc(sem("qi_staged"), 1)

            def stage_values(h):
                pool.wait_ge(sem("o_done"), h + 1)
                pool.tensor_copy(v_st[:, :, :], v_dsa[:, :, ds(h * HD, HD)]).then_inc(sem("v_staged"), 1)

            pool.wait_ge(sem("tile_out0"), c.at("v_dsa"))
            pool.wait_ge(sem("tile_out1"), c.at("v_dsa"))
            with c.loop(pool, "dsa", H_DSA - 1) as i:
                stage_values(i)
                pool.wait_ge(sem("x_done"), i + 2)
                load(w_uk_st[:, :], a["w_uk"][ds((i + 1) * HD, HD), :], "uk")
            stage_values(H_DSA - 1)

            def stage_heads(name, n, q_src, v_src):
                with c.loop(pool, name, n) as i:
                    pool.wait_ge(sem("s_done"), i + c.at(name + "s"))
                    pool.tensor_copy(q_st[:, :], flat(q_src[:, ds(i, 1), :])).then_inc(sem("q_staged"), 1)
                    pool.wait_ge(sem("o_done"), i + c.at(name + "o"))
                    pool.tensor_copy(v_st[:, :, :], v_src[:, :, ds(i * HD, HD)]).then_inc(sem("v_staged"), 1)

            def merge(name, merged, gate, tiles):
                with c.loop(pool, name, D // NB) as i:
                    cols = ds(i * NB, NB)
                    for r in range(R):
                        pool.wait_ge(sem(f"tile_out{r}"), i + tiles + 1)
                        ins = pool.tensor_tensor(merged[:, r, cols], merged[:, r, cols], gate[:, r, cols], ALU.add)
                    ins.then_inc(sem("summed"), 1)
                    c.next("summed")

            stage_heads("moba", H_MOBA, qkm_t[:, 0:H_MOBA, :], vm)
            merge("merge_b", gate_a, gate_b, c.at("ups_b"))
            c.mark("summed1", "summed")
            pool.wait_ge(sem("tile_out1"), c.at("merged"))
            load(x_res[:, :, :], a["x"].rearrange("(r p) n -> p r n", p=P), "x_res")
            load(vec_a[:, :], rows(a["ln_g"][0, :]), "vec")
            load(vec_b[:, :], rows(a["ln_b"][0, :]), "vec")
            pool.wait_ge(sem("tp_free"), c.at("fed"))
            load(mem_nat[:, :, :], a["mem"].rearrange("(r p) n -> p r n", p=P), "mem")
            load(g_col[:, :], a["norm_g"].rearrange("(t p) -> p t", p=P), "small2",
                 allow_slow_non_contiguous=True)
            load(qk_g[:, :], a["qk_norm_g"].rearrange("n p -> p n"), "small2",
                 allow_slow_non_contiguous=True)
            load(bf_v[:, :], rows(a["b_f"]), "small2")
            load(wf[:, :, :], a["w_in_2"][:, C_F:C_F + H_B2].rearrange("(t p) n -> p t n", p=P), "small2")
            pool.memset(upto[:, :, :], 1.0).then_inc(sem("pool_step"), 1)
            pool.wait_ge(sem("pool_step"), c.next("pool_step"))
            for t in range(R):
                pool.affine_select(out=upto[:, t, :], in_=upto[:, t, :], compare_op=ALU.is_ge, fill=0.0,
                                   base=-t * P, pattern=[[1, S]], channel_multiplier=-1).then_inc(sem("pool_step"), 1)
                pool.wait_ge(sem("pool_step"), c.next("pool_step"))
            for m in range(3):
                pool.wait_ge(sem("norm_ready"), m + 1)
                for n in (2, 3):
                    cols = slice(n * NB, (n + 1) * NB)
                    for r in range(R):
                        x = x_res[:, r, cols]
                        pool.tensor_scalar(x, x, mv[:, r, 0:1], rstd[:, r:r + 1], ALU.subtract, ALU.mult)\
                            .then_inc(sem("pool_step"), 1)
                        c.next("pool_step")
                    for r in range(R):
                        x = x_res[:, r, cols]
                        pool.wait_ge(sem("pool_step"), c.value("pool_step", 1))
                        pool.tensor_tensor(x, x, vec_a[:, cols], ALU.mult).then_inc(sem("pool_step"), 1)
                        c.next("pool_step")
                    for r in range(R):
                        x = x_res[:, r, cols]
                        pool.wait_ge(sem("pool_step"), c.value("pool_step", 1 - r))
                        ins = pool.tensor_tensor(x, x, vec_b[:, cols], ALU.add)
                    ins.then_inc(sem("late_chunk"), 1)
                pool.wait_ge(sem("chunk"), 3 * (m + 1))
                pool.wait_ge(sem("late_chunk"), 2 * (m + 1))
                if m < 2:
                    load(vec_a[:, :], rows(a["ln_g"][m + 1, :]), "vec")
                    load(vec_b[:, :], rows(a["ln_b"][m + 1, :]), "vec")
            load(vec_a[:, :], rows(a["b_gate_2"][0, 0:D]), "vec")
            pool.wait_ge(sem("ext"), 32)
            for n in range(3):
                pool.wait_ge(sem("tp_free"), c.at(f"q2_{n}"))
                pool.wait_ge(sem("tile_out1"), c.at(f"v2_{n}"))
                stage_heads(f"branch{n}", H_B2, q2_t if n < 2 else k2_t, v2)
                if n < 2:
                    pool.wait_ge(sem("tile_out1"), c.at(f"gates2_{n}"))
                    load(vec_a[:, :], rows(a["b_gate_2"][0, (n + 1) * D:(n + 2) * D]), "vec")
                if n == 0:
                    pool.wait_ge(sem("s_read"), c.at("forget"))
                    for h in range(H_B2):
                        for lo, hi in TILE_COLS:
                            src = bass.AP(tensor=ext.tensor, offset=ext.offset + h * (2 * S - 1) + P,
                                          ap=[[1, P], [1, hi - lo]])
                            load(bias4[:, h, lo:hi], src, "rel")
                else:
                    merge(f"merge{n}", merged2, gate2, c.at(f"ups{n}"))
                    c.mark(f"summed_b{n}", "summed")

        @block.tensor
        def _(pe):
            c = Counts("pe", per)
            mm, T = nc.tensor.matmul, nc.tensor.transpose

            def group(kt, first, last, hi, lo, n=NB):
                slot = (c.base.get("g", 0) + c.local.get("g", 0)) % SLOTS
                pe.wait_ge(sem("lo_done"), c.next("lo_done"))
                for r in range(R):
                    if first and some(c.value(f"tile_out{r}")):
                        pe.wait_ge(sem(f"tile_out{r}"), c.value(f"tile_out{r}"))
                    for t in range(GK):
                        rows = slice(r * P, (r + 1) * P)
                        for k, (x, w) in enumerate(((hi, w_hi), (hi, w_lo), (lo, w_hi))):
                            ins = mm(ps[:, ACC + r, 0:n], x[:, kt + t, rows], w[:, slot, t, 0:n],
                                     start=first and t == 0 and k == 0, stop=last and t == GK - 1 and k == 2)
                    if r == 1:
                        ins.then_inc(sem("w_used"), 1)
                    elif last:
                        ins.then_inc(sem("tile0_done"), 1)
                c.next("g")

            def weights(kts=KT, hi=x_hi, lo=x_lo, n=NB, hook=None, before=None):
                groups = kts // GK
                for j in range(groups):
                    if before:
                        before(j)
                    group(j * GK, j == 0, j == groups - 1, hi, lo, n)
                    if hook:
                        hook(j)
                for r in range(R):
                    c.next(f"tile_out{r}")

            def turn(ready):
                pe.wait_ge(sem("tp_free"), c.value("tp_free"))
                for r in range(R):
                    ready(r)
                    for j in range(4):
                        ins = T(ps[:, TP + j // 2, (j % 2) * S + r * P:(j % 2) * S + (r + 1) * P],
                                nat[:, r, j * P:(j + 1) * P], ident[:, :])
                        if r == 1 and j % 2:
                            ins.then_inc(sem("tp_done"), 1)
                c.next("tp_free", 2)

            def left(r):
                pe.wait_ge(sem(f"tile_out{r}"), c.value(f"tile_out{r}"))

            def nat_ready(r):
                if r == 0:
                    pe.wait_ge(sem("nat_ready"), c.next("nat_ready"))

            def feed_batch(src, t):
                for kk in range(2):
                    for r in range(R):
                        ins = T(ps[:, TP + t % 2, kk * S + r * P:kk * S + (r + 1) * P],
                                src[:, r, (2 * t + kk) * P:(2 * t + kk + 1) * P], ident[:, :])
                ins.then_inc(sem("tp_done"), 1)
                c.next("tp_free")

            def feed_weights(src, ready, **how):
                pe.wait_ge(sem("tp_free"), c.value("tp_free"))
                for t in range(2):
                    ready(t)
                    feed_batch(src, t)
                last = how.pop("hook", None)

                def before(j):
                    issued = min(j + 2, KT // 2)
                    pe.wait_ge(sem("tp_free"), c.value("tp_free", issued - j - 1))

                def after(j):
                    if j + 2 < KT // 2:
                        ready(j + 2)
                        feed_batch(src, j + 2)
                    if last:
                        last(j)
                weights(before=before, hook=after, **how)

            def normed(m):
                def by_chunk(t):
                    if t < 3:
                        pe.wait_ge(sem("chunk"), 3 * m + t + 1)
                    elif t in (4, 6):
                        pe.wait_ge(sem("late_chunk"), 2 * m + t // 2 - 1)
                return by_chunk

            def scores(pairs):
                pe.wait_ge(sem("s_read"), c.value("s_read"))
                for t, (lo, hi) in enumerate(TILE_COLS):
                    for k, (q, keys) in enumerate(pairs):
                        ins = mm(ps[:, SC, lo:hi], q[:, t * P:(t + 1) * P], keys(hi - lo),
                                 start=k == 0, stop=k == len(pairs) - 1)
                ins.then_inc(sem("s_done"), 1)
                c.next("s_read")

            def turn_probs():
                pe.wait_ge(sem("p_ready"), c.next("p_ready"))
                pe.wait_ge(sem("pt_ready"), c.value("pt_ready"))
                for j in range(3):
                    ins = T(ps[:, PT, j * P:(j + 1) * P], logits[:, 0, j * P:(j + 1) * P], ident[:, :])
                ins.then_inc(sem("t_done"), 1)
                c.next("pt_ready")

            def weigh(bank, col, v0, v1):
                mm(ps[:, bank, col:col + S], v0, probs_t[:, 0:S], start=True, stop=False)
                return mm(ps[:, bank, col + P:col + S], v1, probs_t[:, S:CW], start=False, stop=True)

            def outputs():
                pe.wait_ge(sem("pt_ready"), c.value("pt_ready"))
                pe.wait_ge(sem("o_free"), c.value("o_free"))
                pe.wait_ge(sem("v_staged"), c.next("v_staged"))
                weigh(OT, 0, v_st[:, 0, :], v_st[:, 1, :]).then_inc(sem("o_done"), 1)
                c.next("o_free")

            for name in TOKENS["pe"]:
                pe.nop().then_inc(sem(name), 1)
            pe.wait_ge(sem("ident"), 1)

            def x_landed(t):
                if t % 2 == 0:
                    pe.wait_ge(sem(f"x_in{t // 2}"), 16)
            feed_weights(x_in, x_landed, n=FIRST_W)
            with c.loop(pe, "q_idx", 2):
                weights()
                turn(left)
            pe.wait_ge(sem("tp_free"), c.value("tp_free"))
            pe.wait_ge(sem("nat_ready"), c.next("nat_ready", 2))
            for r in range(R):
                T(ps[:, TP, r * P:(r + 1) * P], kidx2[:, r, :], ident[:, :])
            T(ps[:, TP, S:S + P], kidx2[:, 0, :], ident[:, :]).then_inc(sem("tp_done"), 1)
            for r in range(R):
                for ct in range(2):
                    ins = T(ps[:, TP + 1, ct * S + r * P:ct * S + (r + 1) * P],
                            lat_nat[:, r, ct * P:(ct + 1) * P], ident[:, :])
            ins.then_inc(sem("tp_done"), 1)
            c.next("tp_free", 2)
            with c.loop(pe, "q_dsa", 2):
                weights()
                turn(left)
            with c.loop(pe, "qk_m", 4):
                pe.wait_ge(sem("qi_staged"), c.next("qi_staged"))

                def index_head(j):
                    if j % 2:
                        return
                    n = j // 2
                    half = slice((n % 2) * IDX_D, (n % 2 + 1) * IDX_D)
                    pe.wait_ge(sem("idx_read"), c.value("idx_read"))
                    for t, (lo, hi) in enumerate(TILE_COLS):
                        ins = mm(ps[:, AUX, lo:hi], qi_st[half, n // 2, t * P:(t + 1) * P],
                                 kidx_t[half, 0:hi - lo], start=True, stop=True)
                    ins.then_inc(sem("idx_done"), 1)
                    c.next("idx_read")
                weights(hook=index_head)
                turn(left)
            for b in range(2):
                weights()
            pe.wait_ge(sem("idx_read"), c.value("idx_read"))
            pe.wait_ge(sem("lat_lo"), 1)
            for b in range(H_DSA * HD // NB):
                weights(kts=GK, hi=lat_hi, lo=lat_lo)

            with c.loop(pe, "dsa", 4) as i:
                def query_latent(h):
                    pe.wait_ge(sem("uk"), c.next("uk", 16))
                    pe.wait_ge(sem("x_ready"), c.value("x_ready"))
                    for ct in range(2):
                        ins = mm(ps[:, AUX, ct * S:(ct + 1) * S], w_uk_st[:, ct * P:(ct + 1) * P],
                                 qd_t[:, ds(h, 1), :], start=True, stop=True)
                    ins.then_inc(sem("x_done"), 1)
                    c.next("x_ready")

                def lat_scores():
                    pe.wait_ge(sem("x_ready"), c.value("x_ready"))
                    scores([(aux_a[:, ct * S:(ct + 1) * S], lambda n, ct=ct: lat_t[:, ct, 0:n])
                            for ct in range(2)])

                def dsa(j):
                    if j == 0:
                        query_latent(i * 2)
                    elif j == 1:
                        lat_scores()
                    elif j == 2:
                        query_latent(i * 2 + 1)
                    elif j == 3:
                        turn_probs()
                    elif j == 4:
                        outputs()
                        lat_scores()
                    elif j == 6:
                        turn_probs()
                    elif j == 7:
                        outputs()
                weights(hook=dsa)
            pe.wait_ge(sem("o_free"), c.value("o_free"))
            with c.loop(pe, "up_a", 4):
                weights(kts=8, hi=oh, lo=ol)
            km_t = qkm_t[:, H_MOBA:, :]
            with c.loop(pe, "moba", 4) as i:
                def head_scores(h, keys):
                    pe.wait_ge(sem("q_staged"), c.next("q_staged"))
                    scores([(q_st, lambda n: keys[:, ds(h, 1), 0:n])])

                def moba(j):
                    if j in (0, 3):
                        head_scores(i * 2 + (j == 3), km_t)
                    if j in (2, 5):
                        turn_probs()
                    if j in (3, 6):
                        outputs()
                def moba_ordered(j):
                    if j == 3:
                        outputs()
                        head_scores(i * 2 + 1, km_t)
                    else:
                        moba(j)
                weights(hook=moba_ordered)
            pe.wait_ge(sem("o_free"), c.value("o_free"))
            with c.loop(pe, "up_b", 4):
                weights(kts=8, hi=oh, lo=ol)

            def merged_by(mark):
                def ready(t):
                    if t % 2 == 0:
                        pe.wait_ge(sem("summed"), max(1, c.at(mark) - D // NB + t // 2 + 1))
                return ready
            feed_weights(gate_a, merged_by("summed1"))
            with c.loop(pe, "w_out", 3):
                weights()

            pe.wait_ge(sem("mem"), 16)
            feed_weights(mem_nat, lambda t: None, hi=mem_hi, lo=mem_lo)
            turn(left)
            weights(hi=mem_hi, lo=mem_lo)
            feed_weights(x_res, normed(0))
            turn(left)
            pe.wait_ge(sem("tp_free"), c.value("tp_free"))
            for r in range(R):
                pe.wait_ge(sem(f"tile_out{r}"), c.value(f"tile_out{r}"))

            pe.wait_ge(sem("s_read"), c.value("s_read"))
            for h in range(H_MEM):
                for r in range(R):
                    ins = mm(ps[:, MEM_SC[h], r * S:(r + 1) * S], qmem_t[:, h, r * P:(r + 1) * P],
                             kmem_t[:, h, :], start=True, stop=True)
                ins.then_inc(sem("s_done"), 1)
                c.next("s_read")

            def mem_turn(h):
                pe.wait_ge(sem("p_ready"), c.next("p_ready"))
                for kt in range(2):
                    for r in range(R):
                        ins = T(ps[:, MEM_PT[h], kt * S + r * P:kt * S + (r + 1) * P],
                                mem_exp[h][:, r * S + kt * P:r * S + (kt + 1) * P], ident[:, :])
                ins.then_inc(sem("t_done"), 1)

            mem_turn(0)
            for h in range(H_MEM):
                if h + 1 < H_MEM:
                    mem_turn(h + 1)
                pe.wait_ge(sem("pt_ready"), c.next("pt_ready"))
                pe.wait_ge(sem("o_free"), c.value("o_free", 1))
                for kt in range(2):
                    ins = mm(mem_out[h], vmem[:, kt, h * HD:(h + 1) * HD],
                             mem_pt[h][:, kt * S:(kt + 1) * S], start=kt == 0, stop=kt == 1)
                ins.then_inc(sem("o_done"), 1)
                c.next("o_free")
            pe.wait_ge(sem("o_free"), c.value("o_free"))
            for b in range(4):
                weights(kts=4, hi=om_h, lo=om_l)

            def turn_last(j):
                if j == 0:
                    turn(left)
            for f0, nf in FFN_PARTS:
                if f0 == 0:
                    feed_weights(x_res, normed(1))
                else:
                    weights()
                weights()
                with c.loop(pe, f"ffn_in{f0}", nf - 1):
                    weights(hook=turn_last)
                    weights()
                turn(left)
                pe.wait_ge(sem("tp_free"), c.value("tp_free"))
                if nf == 4:
                    with c.loop(pe, f"ffn_out{f0}", 4):
                        weights(kts=4 * nf, hi=ff_h, lo=ff_l)
                else:
                    with c.loop(pe, f"ffn_out{f0}", 2):
                        for b in range(2):
                            weights(kts=4 * nf, hi=ff_h, lo=ff_l)

            def forget_logits(j):
                if j < KT // GK - 1:
                    return
                pe.wait_ge(sem("wf_split"), 1)
                for kt in range(KT):
                    for x in (x_hi, x_lo):
                        ins = mm(ps[0:2 * H_B2, AUX, 0:S], wf2[:, kt, :], x[:, kt, :],
                                 start=kt == 0 and x is x_hi, stop=kt == KT - 1 and x is x_lo)
                ins.then_inc(sem("f_done"), 1)

            for n in range(3):
                def turn_at_3(j):
                    if j == 3:
                        turn(nat_ready)

                    if n == 0 and j == 4:
                        pe.wait_ge(sem("f_nat"), 1)
                        for r in range(R):
                            ins = T(ps[:, AUX, S + r * 8:S + (r + 1) * 8], f_t[:, r * P:(r + 1) * P],
                                    ident[0:2 * H_B2, 0:2 * H_B2])
                        ins.then_inc(sem("f_done"), 1)

                def turn_raw(j):
                    if j == 3:
                        turn(left)

                def forget_at(j):
                    if n == 0 and j == 0:
                        pe.wait_ge(sem("logf_ready"), 1)
                        mm(ps[:, AUX, 0:4], upto[:, 0, 0:P], logf[:, 0, :], start=True, stop=True)
                        mm(ps[:, AUX, 4:8], upto[:, 0, P:S], logf[:, 0, :], start=True, stop=False)
                        mm(ps[:, AUX, 4:8], upto[:, 1, P:S], logf[:, 1, :], start=False, stop=True)\
                            .then_inc(sem("f_done"), 1)
                    if n == 0 and j % 2 == 1:
                        pe.wait_ge(sem("ck_in"), c.next("ck_in"))
                        for t in range(R):
                            ins = mm(ps[:, AUX, 0:S], ones[:, :], aux_a[:, t * S:(t + 1) * S],
                                     start=t == 0, stop=t == 1)
                        ins.then_inc(sem("f_done"), 1)
                    if j == 3:
                        turn(left)

                def turn_k(j):
                    if j == 3:
                        turn(nat_ready if n < 2 else left)

                if n == 0:
                    feed_weights(x_res, normed(2), hook=forget_logits)
                else:
                    weights()
                weights(hook=turn_at_3 if n < 2 else turn_raw)
                weights(hook=turn_k)
                weights(hook=forget_at)
                pe.wait_ge(sem("tp_free"), c.value("tp_free"))
                with c.loop(pe, f"branch{n}", 4) as i:
                    def soft(j):
                        if j == 0:
                            pe.wait_ge(sem("q_staged"), c.next("q_staged"))
                            scores([(q_st, lambda m: k2_t[:, ds(i, 1), 0:m])])
                        if j == 3:
                            turn_probs()
                        if j == 5:
                            outputs()

                    def stick(j):
                        if j == 0:
                            pe.wait_ge(sem("q_staged"), c.next("q_staged"))
                            pe.wait_ge(sem("s_read"), c.value("s_read"))
                            for t, (lo, hi) in enumerate(((0, S), (S, CW))):
                                ins = mm(ps[:, SC, lo:hi], q_st[:, t * P:(t + 1) * P],
                                         q2_t[:, ds(i, 1), t * P:S], start=True, stop=True)
                            ins.then_inc(sem("s_done"), 1)
                            c.next("s_read")
                        if j == 3:
                            pe.wait_ge(sem("p_ready"), c.next("p_ready"))
                            mm(ps[:, PT, 0:S], lower[:, :], aux_b[:, 0:S], start=True, stop=False)
                            mm(ps[:, PT, P:S], ones[:, :], aux_b[:, S:CW], start=False, stop=True)
                            mm(ps[:, PT, S:CW], lower[:, :], aux_b[:, S:CW], start=True, stop=True)\
                                .then_inc(sem("t_done"), 1)
                            c.next("pt_ready")
                        if j == 5:
                            outputs()
                    weights(hook=soft if n < 2 else stick)
                pe.wait_ge(sem("o_free"), c.value("o_free"))
                with c.loop(pe, f"up2_{n}", 2):
                    for b in range(2):
                        weights(kts=4, hi=y_h, lo=y_l)
            feed_weights(merged2, merged_by("summed_b2"))
            for b in range(3):
                weights()

        @block.scalar
        def _(act):
            c = Counts("act", per)

            def split():
                g = c.value("hi")
                if isinstance(g, int) and g >= N_GROUPS:
                    return
                slot = (c.base.get("hi", 0) + c.local.get("hi", 0)) % SLOTS
                parts = 2 if isinstance(g, int) and (g < KT // GK or G_UV <= g < G_UV + H_DSA * HD // NB) else 1
                act.wait_ge(sem(f"landed{slot}"), c.next(f"landed{slot}", 16 * parts))
                used = c.value("hi", SLOTS - 1)
                if some(used):
                    act.wait_ge(sem("w_used"), used)
                n = width(g)
                act.activation(w_hi[:, slot, :, 0:n], stage[:, slot, :, 0:n], ACT.Copy)\
                   .then_inc(sem("hi"), 1)
                c.next("hi")

            def weights(kts=KT, hook=None):
                groups = kts // GK
                for j in range(groups):
                    for _ in range(1 if groups == 1 else 2 if j == 0 else 0 if j == groups - 1 else 1):
                        split()
                    c.next("w_used")
                    if hook:
                        hook(j)

            def tile_done(r):
                if r == 0:
                    act.wait_ge(sem("tile0_done"), c.next("tile0_done"))
                else:
                    act.wait_ge(sem("w_used"), c.value("w_used"))

            def evac(dst, func=ACT.Copy, nat_free=True, scale=None):
                for r in range(R):
                    tile_done(r)
                    if r == 0 and nat_free:
                        act.wait_ge(sem("tp_done"), c.value("tp_done"))
                    by = 1.0 if scale is None else scale[:, r:r + 1]
                    act.activation(dst(r), ps[:, ACC + r, :], func, scale=by).then_inc(sem(f"tile_out{r}"), 1)
                    c.next(f"tile_out{r}")

            def to_nat(func=ACT.Copy, scale=None):
                evac(lambda r: nat[:, r, :], func, scale=scale)

            def skip_block():
                c.next("tile0_done")
                for r in range(R):
                    c.next(f"tile_out{r}")

            def hi_batch(dst, t, scale=None):
                act.wait_ge(sem("tp_done"), c.next("tp_done"))
                if scale is None:
                    ins = act.activation(dst, ps[:, TP + t % 2, :].rearrange("p (k s) -> p k s", k=2), ACT.Copy)
                else:
                    for k in range(2):
                        ins = act.activation(dst[:, k, :], ps[:, TP + t % 2, k * S:(k + 1) * S], ACT.Identity,
                                             scale=scale[:, 2 * t + k:2 * t + k + 1])
                ins.then_inc(sem("hi_t"), 1)

            def hi_part(dst, n):
                for t in range(n):
                    hi_batch(dst(t), t)

            def feed_weights(dst, scale=None, hook=None):
                for t in range(2):
                    hi_batch(dst[:, 2 * t:2 * t + 2, :], t, scale)

                def after(j):
                    if j + 2 < KT // 2:
                        hi_batch(dst[:, 2 * j + 4:2 * j + 6, :], j + 2, scale)
                    if hook:
                        hook(j)
                weights(hook=after)

            def root(x):
                act.wait_ge(sem("var"), c.next("var"))
                act.activation(x, x, ACT.Sqrt).then_inc(sem("root"), 1)

            def exps():
                act.wait_ge(sem("nmax"), c.next("nmax"))
                c.next("s_read")
                for t, (lo, hi) in enumerate(TILE_COLS):
                    ins = act.activation(logits[:, 0, lo:hi], logits[:, 0, lo:hi], ACT.Exp,
                                         bias=nmax[:, t:t + 1], accum_out=rsum[:, t:t + 1])
                ins.then_inc(sem("exp_done"), 1)

            def probs_out(used):
                act.wait_ge(sem("t_done"), c.next("t_done"))
                act.wait_ge(sem(used), c.value(used))
                act.activation(probs_t[:, 0:CW], ps[:, PT, 0:CW], ACT.Copy).then_inc(sem("pt_ready"), 1)

            def out_hi(dst):
                act.wait_ge(sem("o_done"), c.next("o_done"))
                act.activation(dst, ps[:, OT, 0:S], ACT.Copy).then_inc(sem("oh_done"), 1)

            for name in TOKENS["act"]:
                act.nop().then_inc(sem(name), 1)
            for _ in range(AHEAD):
                split()
            feed_weights(x_hi)
            skip_block()
            root(sd[:, 0:R])
            root(sd[:, 0:R])
            with c.loop(act, "q_idx", 2):
                weights()
                to_nat()
                c.next("tp_done", 2)
            c.next("tp_done", 2)
            with c.loop(act, "q_dsa", 2):
                weights()
                to_nat()
                c.next("tp_done", 2)
            with c.loop(act, "qk_m", 4):
                def index_head(j):
                    if j % 2 == 0:
                        act.wait_ge(sem("idx_done"), c.next("idx_done"))
                        act.wait_ge(sem("relu_used"), c.value("relu_used"))
                        act.activation(relu_s[:, :], ps[:, AUX, 0:CW], ACT.Relu).then_inc(sem("idx_read"), 1)
                        c.next("relu_used")
                weights(hook=index_head)
                to_nat()
                c.next("tp_done", 2)
            for b in range(2):
                def latent_hi(j):
                    if b == 0 and j == 0:
                        act.activation(lat_hi, lat_t[:, :, :], ACT.Copy).then_inc(sem("lat_hi"), 1)
                weights(hook=latent_hi)
                evac(lambda r: vm[:, r, b * NB:(b + 1) * NB])
            for b in range(H_DSA * HD // NB):
                weights(kts=GK)
                evac(lambda r: v_dsa[:, r, b * NB:(b + 1) * NB])
            c.mark("v_dsa", "tile_out1")
            tiles_a = c.value("tile_out1")
            with c.loop(act, "dsa", 4) as i:
                def aux_out(dst, used):
                    act.wait_ge(sem("x_done"), c.next("x_done"))
                    act.wait_ge(sem(used), c.value(used))
                    act.activation(dst[:, :], ps[:, AUX, :], ACT.Copy).then_inc(sem("x_ready"), 1)

                def dsa(j):
                    if j in (0, 2):
                        aux_out(aux_a, "s_done")
                    elif j in (1, 4):
                        if j == 4:
                            out_hi(flat(oh[:, ds(i * 2, 1), :]))
                        c.next("s_done")
                        exps()
                    elif j in (3, 6):
                        probs_out("o_done")
                    elif j == 7:
                        out_hi(flat(oh[:, ds(i * 2 + 1, 1), :]))
                weights(hook=dsa)
                skip_block()

            def up(name, gate, tiles):
                with c.loop(act, name, 4) as i:
                    g = gate[:, :, ds(i * NB, NB)]
                    for r in range(R):
                        act.wait_ge(sem(f"tile_out{r}"), i + tiles + 1)
                    act.activation(g, g, ACT.Sigmoid).then_inc(sem("gate_ready"), 1)
                    weights(kts=8)
                    skip_block()
            up("up_a", gate_a, tiles_a)
            tiles_b = c.value("tile_out1")
            with c.loop(act, "moba", 4) as i:
                def moba(j):
                    if j in (0, 3):
                        if j == 3:
                            out_hi(flat(oh[:, ds(i * 2, 1), :]))
                        exps()
                    if j in (2, 5):
                        probs_out("o_done")
                    if j == 6:
                        out_hi(flat(oh[:, ds(i * 2 + 1, 1), :]))
                weights(hook=moba)
                skip_block()
            up("up_b", gate_b, tiles_b)
            feed_weights(x_hi)
            skip_block()
            with c.loop(act, "w_out", 3):
                weights()
                skip_block()
            feed_weights(mem_hi)
            to_nat()
            c.next("tp_done", 2)

            def ln_root(j):
                if j == 0:
                    root(sd[:, 0:R])
            weights(hook=ln_root)
            evac(lambda r: vmem[:, r, :])
            feed_weights(x_hi)
            to_nat()
            c.next("tp_done", 2)

            def mem_exps(h):
                act.wait_ge(sem("nmax"), c.next("nmax"))
                for r in range(R):
                    ins = act.activation(mem_exp[h][:, r * S:(r + 1) * S],
                                         ps[:, MEM_SC[h], r * S:(r + 1) * S], ACT.Exp, scale=SCALE,
                                         bias=mem_max[:, h, r:r + 1], accum_out=mem_sum[:, h, r:r + 1])
                ins.then_inc(sem("s_read"), 1)
                c.next("s_read")

            def mem_probs(h):
                act.wait_ge(sem("t_done"), c.next("t_done"))
                act.activation(mem_pt[h][:, :], ps[:, MEM_PT[h], :], ACT.Copy).then_inc(sem("pt_ready"), 1)

            def mem_upper(h):
                act.wait_ge(sem("o_done"), c.next("o_done"))
                act.activation(om_h[:, h, :], mem_out[h], ACT.Copy).then_inc(sem("oh_done"), 1)

            act.wait_ge(sem("t_done"), c.value("t_done"))
            for piece, h in ((mem_exps, 0), (mem_exps, 1), (mem_exps, 2), (mem_probs, 0), (mem_exps, 3),
                             (mem_probs, 1), (mem_upper, 0), (mem_probs, 2), (mem_upper, 1), (mem_probs, 3),
                             (mem_upper, 2), (mem_upper, 3)):
                piece(h)
            for b in range(4):
                weights(kts=4)
                skip_block()
            root(sd[:, 0:R])
            def hidden(feeding=False, hook=None):
                if feeding:
                    feed_weights(x_hi)
                else:
                    weights(hook=hook)
                evac(lambda r: silu_g[:, r, :], ACT.Silu, nat_free=False)
                weights()
                skip_block()

            def product_hi(i):
                hi_part(lambda t: ff_h[:, ds(i * 4 + 2 * t, 2), :], 2)

            for f0, nf in FFN_PARTS:
                hidden(feeding=f0 == 0)
                with c.loop(act, f"ffn_in{f0}", nf - 1) as i:
                    hidden(hook=lambda j: product_hi(i) if j == 0 else None)
                product_hi(nf - 1)
                if nf == 4:
                    with c.loop(act, f"ffn_out{f0}", 4):
                        weights(kts=4 * nf)
                        skip_block()
                else:
                    with c.loop(act, f"ffn_out{f0}", 2):
                        for b in range(2):
                            weights(kts=4 * nf)
                            skip_block()
            root(sd[:, 0:R])
            act.wait_ge(sem("small2"), 64)
            act.activation(wf2[:, :, 0:H_B2], wf[:, :, :], ACT.Copy).then_inc(sem("wf_hi"), 1)

            def squares(j):
                if j % 2 == 0:
                    return
                n = j // 2
                if n < 2:
                    act.wait_ge(sem("chunk"), 3 * 2 + n + 2)
                else:
                    act.wait_ge(sem("late_chunk"), 2 * 2 + n - 1)
                if n == 0:
                    act.wait_ge(sem("t_done"), c.value("t_done"))
                for r in range(R):
                    ins = act.activation(logits[:, r, :], x_res[:, r, n * NB:(n + 1) * NB], ACT.Square,
                                         accum_out=ssq[:, r * 4 + n:r * 4 + n + 1])
                    ins.then_inc(sem("squares"), 1)
                    act.wait_ge(sem("squares"), c.next("squares"))

            def log1p_exp(x, src, count):
                act.wait_ge(sem(count), c.next(count))
                act.activation(x, src, ACT.Abs).then_inc(sem("act_step"), 1)
                act.wait_ge(sem("act_step"), c.next("act_step"))
                act.activation(x, x, ACT.Exp, scale=-1.0).then_inc(sem("act_step"), 1)
                act.wait_ge(sem("act_step"), c.next("act_step"))
                act.activation(x, x, ACT.Ln, bias=1.0).then_inc(sem("ln_done"), 1)

            for n in range(3):
                def q_norm(j):
                    if n < 2 and j == 0:
                        root(sd[:, :])
                if n == 0:
                    feed_weights(x_hi, g_col, squares)
                    root(rms[:, :])
                    act.wait_ge(sem("rms_ready"), 1)
                else:
                    weights()
                to_nat(ACT.Identity, rms)
                c.next("tp_done", 2)

                def k_hook(j):
                    q_norm(j)
                    if n == 0 and j == 5:
                        c.next("az", 3)
                        log1p_exp(f_b[:, :, :], f_a[:, :, :], "az")
                weights(hook=k_hook)
                to_nat(ACT.Identity, rms)
                c.next("tp_done", 2)
                weights(hook=q_norm)
                to_nat(ACT.Silu, rms)
                c.next("tp_done", 2)
                weights()
                evac(lambda r: v2[:, r, :], ACT.Identity, nat_free=False, scale=rms)
                tiles = c.value("tile_out1")
                with c.loop(act, f"branch{n}", 4) as i:
                    def soft(j):
                        if j == 0:
                            exps()
                        if j == 3:
                            probs_out("o_done")

                    def stick(j):
                        if j == 0:
                            log1p_exp(aux_b[:, 0:CW], logits[:, 1, 0:CW], "s_read")
                        if j == 3:
                            c.next("t_done")
                            act.wait_ge(sem("nmax"), c.next("nmax"))
                            act.wait_ge(sem("o_done"), c.value("o_done"))
                            act.activation(probs_t[:, 0:CW], logits[:, 0, 0:CW], ACT.Exp)\
                               .then_inc(sem("pt_ready"), 1)

                    def both(j):
                        (soft if n < 2 else stick)(j)
                        if j == 5:
                            c.next("o_done")
                            act.wait_ge(sem("y_ready"), c.next("y_ready"))
                            act.activation(flat(y_h[:, ds(i, 1), :]), aux_a[:, 0:S], ACT.Copy)\
                               .then_inc(sem("oh_done"), 1)
                    weights(hook=both)
                    skip_block()
                with c.loop(act, f"up2_{n}", 2) as i:
                    for b in range(2):
                        g = gate2[:, :, ds((i * 2 + b) * NB, NB)]
                        for r in range(R):
                            act.wait_ge(sem(f"tile_out{r}"), i * 2 + (tiles + b + 1))
                        act.activation(g, g, ACT.Sigmoid).then_inc(sem("gate_ready"), 1)
                        weights(kts=4)
                        skip_block()
            feed_weights(x_hi)
            skip_block()
            for b in range(3):
                weights()
                skip_block()

        @block.vector
        def _(dve):
            c = Counts("dve", per)

            def split():
                g = c.value("lo_done")
                if isinstance(g, int) and g >= N_GROUPS:
                    return
                slot = (c.base.get("lo_done", 0) + c.local.get("lo_done", 0)) % SLOTS
                dve.wait_ge(sem("hi"), c.next("hi"))
                n = width(g)
                dve.tensor_tensor(w_lo[:, slot, :, 0:n], stage[:, slot, :, 0:n],
                                  w_hi[:, slot, :, 0:n].bitcast(F32), ALU.subtract).then_inc(sem("lo_done"), 1)
                c.next("lo_done")

            def weights(kts=KT, hook=None):
                groups = kts // GK
                for j in range(groups):
                    for _ in range(1 if groups == 1 else 2 if j == 0 else 0 if j == groups - 1 else 1):
                        split()
                    c.next("w_used")
                    if hook:
                        hook(j)

            def tile_done(r):
                if r == 0:
                    dve.wait_ge(sem("tile0_done"), c.next("tile0_done"))
                else:
                    dve.wait_ge(sem("w_used"), c.value("w_used"))

            def skip_block():
                c.next("tile0_done")
                for r in range(R):
                    c.next(f"tile_out{r}")

            def heads_in(dst, scale=None):
                for t in range(2):
                    dve.wait_ge(sem("tp_done"), c.next("tp_done"))
                    src = ps[:, TP + t, :].rearrange("p (k s) -> p k s", k=2)
                    if scale is None:
                        ins = dve.tensor_copy(dst(t), src)
                    else:
                        ins = dve.tensor_scalar(dst(t), src, scale, None, ALU.mult)
                    ins.then_inc(sem("tp_free"), 1)
                    c.next("tp_free")

            def lo_batch(hi, lo, t, scale=None):
                dve.wait_ge(sem("hi_t"), c.next("hi_t"))
                if scale is None:
                    ins = dve.tensor_tensor(lo, ps[:, TP + t % 2, :].rearrange("p (k s) -> p k s", k=2),
                                            hi.bitcast(F32), ALU.subtract)
                else:
                    for k in range(2):
                        ins = dve.scalar_tensor_tensor(
                            out=lo[:, k, :], in0=ps[:, TP + t % 2, k * S:(k + 1) * S],
                            scalar=scale[:, 2 * t + k:2 * t + k + 1], in1=hi[:, k, :].bitcast(F32),
                            op0=ALU.mult, op1=ALU.subtract)
                ins.then_inc(sem("tp_free"), 1)
                c.next("tp_done")
                c.next("tp_free")

            def lo_part(hi, lo, n):
                for t in range(n):
                    lo_batch(hi(t), lo(t), t)

            def feed_weights(hi, lo, scale=None, norm=None):
                def batch(t):
                    lo_batch(hi[:, 2 * t:2 * t + 2, :], lo[:, 2 * t:2 * t + 2, :], t, scale)
                if norm:
                    norm(0)
                for t in range(2):
                    batch(t)
                if norm:
                    norm(1)
                weights(hook=lambda j: batch(j + 2) if j + 2 < KT // 2 else None)

            def inverse_root(x, n, mean, eps):
                dve.tensor_scalar(sd[:, 0:n], x, mean, eps, ALU.mult, ALU.add).then_inc(sem("var"), 1)
                dve.wait_ge(sem("root"), c.next("root"))
                dve.reciprocal(rstd[:, 0:n], sd[:, 0:n]).then_inc(sem("dve_step"), 1)
                dve.wait_ge(sem("dve_step"), c.next("dve_step"))

            def logits_in(bias, op=ALU.add):
                dve.wait_ge(sem("s_done"), c.next("s_done"))
                dve.wait_ge(sem("t_done"), c.value("t_done"))
                dve.scalar_tensor_tensor(out=logits[:, 0, 0:CW], in0=ps[:, SC, 0:CW], scalar=SCALE,
                                         in1=bias, op0=ALU.mult, op1=op).then_inc(sem("s_read"), 1)
                dve.wait_ge(sem("s_read"), c.next("s_read"))
                for t, (lo, hi) in enumerate(TILE_COLS):
                    ins = dve.tensor_reduce(nmax[:, t:t + 1], logits[:, 0, lo:hi], AX.X, ALU.max)
                ins.then_inc(sem("dve_step"), 1)
                dve.wait_ge(sem("dve_step"), c.next("dve_step"))
                dve.tensor_scalar(nmax[:, :], nmax[:, :], -1.0, None, ALU.mult).then_inc(sem("nmax"), 1)

            def normalise(tiles, x, ready=("exp_done",)):
                dve.wait_ge(sem(ready[0]), c.next(ready[0]))
                dve.reciprocal(rinv[:, :], rsum[:, :]).then_inc(sem("dve_step"), 1)
                dve.wait_ge(sem("dve_step"), c.next("dve_step"))
                for t, (lo, hi) in enumerate(tiles):
                    ins = dve.tensor_scalar(x[:, lo:hi], x[:, lo:hi], rinv[:, t:t + 1], None, ALU.mult)
                ins.then_inc(sem("p_ready"), 1)

            def softmax(bias, op=ALU.add):
                logits_in(bias, op)
                normalise(TILE_COLS, logits[:, 0, :])

            def out_lo(hi, lo):
                dve.wait_ge(sem("oh_done"), c.next("oh_done"))
                c.next("o_done")
                dve.tensor_tensor(lo, ps[:, OT, 0:S], hi.bitcast(F32), ALU.subtract).then_inc(sem("o_free"), 1)

            def gates_in(gate, vec, i, by=None):
                for r in range(R):
                    tile_done(r)
                    out_, bias = gate[:, r, ds(i * NB, NB)], vec[:, ds(i * NB, NB)]
                    if by is None:
                        ins = dve.tensor_tensor(out_, ps[:, ACC + r, :], bias, ALU.add)
                    else:
                        ins = dve.scalar_tensor_tensor(out=out_, in0=ps[:, ACC + r, :], scalar=by[:, r:r + 1],
                                                       in1=bias, op0=ALU.mult, op1=ALU.add)
                    ins.then_inc(sem(f"tile_out{r}"), 1)
                    c.next(f"tile_out{r}")

            def gated(gate, merged, i, add):
                dve.wait_ge(sem("gate_ready"), c.next("gate_ready"))
                cols = ds(i * NB, NB)
                for r in range(R):
                    tile_done(r)
                    dst = gate if add else merged
                    dve.tensor_tensor(dst[:, r, cols], ps[:, ACC + r, :], gate[:, r, cols], ALU.mult)\
                       .then_inc(sem(f"tile_out{r}"), 1)
                    c.next(f"tile_out{r}")

            def residual(i, alpha, stat):
                cols = ds(i * NB, NB)
                for r in range(R):
                    tile_done(r)
                    x = x_res[:, r, cols]
                    dve.scalar_tensor_tensor(out=x, in0=x, scalar=alpha, in1=ps[:, ACC + r, :],
                                             op0=ALU.mult, op1=ALU.add).then_inc(sem(f"tile_out{r}"), 1)
                    c.next(f"tile_out{r}")
                    if stat:
                        dve.wait_ge(sem(f"tile_out{r}"), c.value(f"tile_out{r}"))
                        dve.bn_stats(flat(stats[:, r, ds(i, 1), :]), x_res[:, r, cols]).then_inc(sem("dve_step"), 1)
                        dve.wait_ge(sem("dve_step"), c.next("dve_step"))

            def centre(cols):
                for r in range(R):
                    x = x_res[:, r, cols]
                    dve.scalar_tensor_tensor(out=x, in0=x, scalar=mv[:, r, 0:1], in1=vec_a[:, cols],
                                             op0=ALU.subtract, op1=ALU.mult).then_inc(sem("dve_step"), 1)
                    c.next("dve_step")

            def rescale(cols):
                for r in range(R):
                    x = x_res[:, r, cols]
                    dve.wait_ge(sem("dve_step"), c.value("dve_step", 1 - r))
                    ins = dve.scalar_tensor_tensor(out=x, in0=x, scalar=rstd[:, r:r + 1], in1=vec_b[:, cols],
                                                   op0=ALU.mult, op1=ALU.add)
                ins.then_inc(sem("chunk"), 1)

            def norm_root(vecs):
                for r in range(R):
                    dve.bn_aggr(mv[:, r, :], flat(stats[:, r, :, :])).then_inc(sem("dve_step"), 1)
                    dve.wait_ge(sem("dve_step"), c.next("dve_step"))
                dve.wait_ge(sem("vec"), vecs)
                dve.tensor_scalar(sd[:, 0:R], mv[:, :, 1], 1.0, LN_EPS, ALU.mult, ALU.add)\
                    .then_inc(sem("var"), 1)
                centre(slice(0, NB // 2))
                dve.wait_ge(sem("root"), c.next("root"))
                dve.reciprocal(rstd[:, 0:R], sd[:, 0:R]).then_inc(sem("norm_ready"), 1)
                dve.wait_ge(sem("norm_ready"), c.next("norm_ready"))
                rescale(slice(0, NB // 2))

            def norm_chunk(n):
                cols = slice(NB // 2, NB) if n == 0 else slice(NB, 2 * NB)
                centre(cols)
                rescale(cols)

            for name in TOKENS["dve"]:
                dve.nop().then_inc(sem(name), 1)
            for _ in range(AHEAD):
                split()
            feed_weights(x_hi, x_lo)
            for r in range(R):
                tile_done(r)
                dve.tensor_copy(lat_nat[:, r, :], ps[:, ACC + r, 0:LAT])
                dve.tensor_copy(kidx2[:, r, 0:IDX_D], ps[:, ACC + r, LAT:LAT + IDX_D])
                dve.tensor_scalar(w_idx[:, r, :], ps[:, ACC + r, LAT + IDX_D:FIRST_W],
                                  IDX_D ** -0.5 * IDX_H ** -0.5, None, ALU.mult)\
                   .then_inc(sem(f"tile_out{r}"), 1)
                dve.wait_ge(sem(f"tile_out{r}"), c.next(f"tile_out{r}"))
                dve.bn_stats(stats[:, r, 0, :], kidx2[:, r, 0:IDX_D]).then_inc(sem("dve_step"), 1)
                dve.wait_ge(sem("dve_step"), c.next("dve_step"))
                dve.bn_aggr(mv[:, r, :], stats[:, r, 0, :]).then_inc(sem("dve_step"), 1)
                dve.wait_ge(sem("dve_step"), c.next("dve_step"))
            inverse_root(mv[:, :, 1], R, 1.0, LN_EPS)
            dve.wait_ge(sem("small"), 48)
            for r in range(R):
                x = kidx2[:, r, 0:IDX_D]
                dve.scalar_tensor_tensor(out=x, in0=x, scalar=mv[:, r, 0:1], in1=ik_g[:, :],
                                         op0=ALU.subtract, op1=ALU.mult).then_inc(sem("dve_step"), 1)
                dve.wait_ge(sem("dve_step"), c.next("dve_step"))
                dve.scalar_tensor_tensor(out=x, in0=x, scalar=rstd[:, r:r + 1], in1=ik_b[:, :],
                                         op0=ALU.mult, op1=ALU.add).then_inc(sem("dve_step"), 1)
                dve.wait_ge(sem("dve_step"), c.next("dve_step"))
                ins = dve.tensor_copy(kidx2[:, r, IDX_D:2 * IDX_D], x)
            ins.then_inc(sem("nat_ready"), 1)
            for r in range(R):
                dve.tensor_tensor(aux_a[:, 0:LAT], lat_nat[:, r, :], lat_nat[:, r, :], ALU.mult)\
                    .then_inc(sem("dve_step"), 1)
                dve.wait_ge(sem("dve_step"), c.next("dve_step"))
                dve.tensor_reduce(ssq[:, r:r + 1], aux_a[:, 0:LAT], AX.X, ALU.add).then_inc(sem("dve_step"), 1)
                dve.wait_ge(sem("dve_step"), c.next("dve_step"))
            inverse_root(ssq[:, 0:R], R, 1.0 / LAT, LN_EPS)
            for r in range(R):
                ins = dve.scalar_tensor_tensor(out=lat_nat[:, r, :], in0=lat_nat[:, r, :],
                                               scalar=rstd[:, r:r + 1], in1=kv_g[:, :],
                                               op0=ALU.mult, op1=ALU.mult)
            ins.then_inc(sem("nat_ready"), 1)
            dve.wait_ge(sem("ext"), 32)
            with c.loop(dve, "q_idx", 2) as i:
                weights()
                skip_block()
                heads_in(lambda t: qi_t[:, ds(i * 4 + 2 * t, 2), :])
            c.mark("q_idx", "tp_free")
            dve.wait_ge(sem("tp_done"), c.next("tp_done"))
            dve.tensor_copy(kidx_t[:, :], ps[:, TP, 0:S]).then_inc(sem("tp_free"), 1)
            dve.wait_ge(sem("tp_done"), c.next("tp_done"))
            dve.tensor_copy(lat_t[:, :, :], ps[:, TP + 1, :].rearrange("p (k s) -> p k s", k=2))\
               .then_inc(sem("tp_free"), 1)
            c.next("tp_free", 2)
            with c.loop(dve, "q_dsa", 2) as i:
                weights()
                skip_block()
                heads_in(lambda t: qd_t[:, ds(i * 4 + 2 * t, 2), :])
            dve.wait_ge(sem("const"), 1)
            with c.loop(dve, "qk_m", 4) as i:
                def index_head(j):
                    if j % 2:
                        return
                    dve.wait_ge(sem("idx_read"), c.next("idx_read"))
                    for t, (lo, hi) in enumerate(TILE_COLS):
                        ins = dve.scalar_tensor_tensor(
                            out=score[:, lo:hi], in0=relu_s[:, lo:hi],
                            scalar=flat(w_idx[:, t:t + 1, ds(i * 4 + j // 2, 1)]),
                            in1=score[:, lo:hi], op0=ALU.mult, op1=ALU.add)
                    ins.then_inc(sem("relu_used"), 1)
                    dve.wait_ge(sem("relu_used"), c.next("relu_used"))
                weights(hook=index_head)
                skip_block()
                heads_in(lambda t: qkm_t[:, ds(i * 4 + 2 * t, 2), :])

            def take8(t, rounds):
                lo, hi = TILE_COLS[t]
                for _ in range(rounds):
                    dve.max(best8[:, :], score[:, lo:hi]).then_inc(sem("dve_step"), 1)
                    dve.wait_ge(sem("dve_step"), c.next("dve_step"))
                    dve.match_replace(out=score[:, lo:hi], in_to_replace=best8[:, :],
                                      in_values=score[:, lo:hi], imm_value=TAKEN).then_inc(sem("dve_step"), 1)
                    dve.wait_ge(sem("dve_step"), c.next("dve_step"))

            dve.tensor_tensor(score[:, :], score[:, :], causal[:, :], ALU.add).then_inc(sem("dve_step"), 1)
            dve.wait_ge(sem("dve_step"), c.next("dve_step"))
            for b in range(2):
                def hook(j):
                    if b == 0 and j == 1:
                        dve.wait_ge(sem("lat_hi"), 1)
                        dve.tensor_tensor(lat_lo, lat_t[:, :, :], lat_hi.bitcast(F32), ALU.subtract)\
                           .then_inc(sem("lat_lo"), 1)
                    take8(b, 1)
                weights(hook=hook)
                skip_block()
            for b in range(H_DSA * HD // NB):
                weights(kts=GK)
                skip_block()
            dve.tensor_scalar(score[:, :], score[:, :], TAKEN / 2, NEG, ALU.is_gt, ALU.mult)\
                .then_inc(sem("dve_step"), 1)
            dve.wait_ge(sem("dve_step"), c.next("dve_step"))
            dve.tensor_tensor(bias_d[:, :], bias_m[:, :], score[:, :], ALU.add).then_inc(sem("dve_step"), 1)
            dve.wait_ge(sem("dve_step"), c.next("dve_step"))

            dve.wait_ge(sem("vec"), 32)
            with c.loop(dve, "dsa", 4) as i:
                def dsa(j):
                    if j == 0:
                        dve.tensor_scalar(bias_d[:, :], bias_d[:, :], 0.5, None, ALU.mult).then_inc(sem("dve_step"), 1)
                        dve.wait_ge(sem("dve_step"), c.next("dve_step"))
                    if j == 4:
                        out_lo(flat(oh[:, ds(i * 2, 1), :]), flat(ol[:, ds(i * 2, 1), :]))
                    if j in (1, 4):
                        softmax(bias_d[:, :])
                    if j in (3, 6):
                        c.next("t_done")
                    if j == 3:
                        dve.tensor_scalar(bias_d[:, :], bias_d[:, :], 0.5, None, ALU.mult).then_inc(sem("dve_step"), 1)
                        dve.wait_ge(sem("dve_step"), c.next("dve_step"))
                    if j == 7:
                        gates_in(gate_a, vec_a, i)
                        out_lo(flat(oh[:, ds(i * 2 + 1, 1), :]), flat(ol[:, ds(i * 2 + 1, 1), :]))
                weights(hook=dsa)
            with c.loop(dve, "up_a", 4) as i:
                weights(kts=8)
                gated(gate_a, gate_a, i, False)
            c.mark("mobas", "s_done")
            c.per[("mark", "mobao")] = 1 + H_DSA
            with c.loop(dve, "moba", 4) as i:
                def moba(j):
                    if j in (0, 3):
                        if j == 3:
                            out_lo(flat(oh[:, ds(i * 2, 1), :]), flat(ol[:, ds(i * 2, 1), :]))
                        dve.tensor_scalar(bias_m[:, :], bias_m[:, :], 0.5, None, ALU.mult).then_inc(sem("dve_step"), 1)
                        dve.wait_ge(sem("dve_step"), c.next("dve_step"))
                        softmax(bias_m[:, :])
                    if j in (2, 5):
                        c.next("t_done")
                    if j == 6:
                        out_lo(flat(oh[:, ds(i * 2 + 1, 1), :]), flat(ol[:, ds(i * 2 + 1, 1), :]))
                    if j == 7:
                        gates_in(gate_b, vec_b, i)
                weights(hook=moba)
            c.mark("ups_b", "tile_out1")
            with c.loop(dve, "up_b", 4) as i:
                weights(kts=8)
                gated(gate_b, gate_a, i, True)
            c.mark("merged", "tile_out1")
            feed_weights(x_hi, x_lo)
            c.mark("fed", "tp_free")
            dve.wait_ge(sem("x_res"), 16)
            residual(0, ALPHA, True)
            with c.loop(dve, "w_out", 3) as i:
                weights()
                residual(i + 1, ALPHA, True)
            feed_weights(mem_hi, mem_lo)
            skip_block()
            heads_in(lambda t: kmem_t[:, 2 * t:2 * t + 2, :])

            def norm_in(j):
                if j == 0:
                    norm_root(64)
                if 1 <= j <= 2:
                    norm_chunk(j - 1)
            weights(hook=norm_in)
            skip_block()
            feed_weights(x_hi, x_lo)
            skip_block()
            heads_in(lambda t: qmem_t[:, 2 * t:2 * t + 2, :])

            def mem_maxima(h):
                dve.wait_ge(sem("s_done"), c.next("s_done"))
                src = ps[:, MEM_SC[h], :].rearrange("p (r k) -> p r k", r=R)
                dve.tensor_reduce(mem_max[:, h, :], src, AX.X, ALU.max).then_inc(sem("dve_step"), 1)
                dve.wait_ge(sem("dve_step"), c.next("dve_step"))
                dve.tensor_scalar(mem_max[:, h, :], mem_max[:, h, :], -SCALE, None, ALU.mult)\
                    .then_inc(sem("nmax"), 1)

            def mem_norm(h):
                dve.wait_ge(sem("s_read"), c.next("s_read"))
                dve.reciprocal(mem_inv[:, h, :], mem_sum[:, h, :]).then_inc(sem("dve_step"), 1)
                dve.wait_ge(sem("dve_step"), c.next("dve_step"))
                for r in range(R):
                    x = mem_exp[h][:, r * S:(r + 1) * S]
                    ins = dve.tensor_scalar(x, x, mem_inv[:, h, r:r + 1], None, ALU.mult)
                ins.then_inc(sem("p_ready"), 1)
                c.next("t_done")

            def mem_rest(h):
                dve.wait_ge(sem("oh_done"), c.next("oh_done"))
                c.next("o_done")
                dve.tensor_tensor(om_l[:, h, :], mem_out[h], om_h[:, h, :].bitcast(F32), ALU.subtract)\
                   .then_inc(sem("o_free"), 1)

            for piece, h in ((mem_maxima, 0), (mem_maxima, 1), (mem_norm, 0), (mem_maxima, 2), (mem_norm, 1),
                             (mem_maxima, 3), (mem_norm, 2), (mem_norm, 3), (mem_rest, 0), (mem_rest, 1),
                             (mem_rest, 2), (mem_rest, 3)):
                piece(h)
            for b in range(4):
                weights(kts=4)
                residual(b, ALPHA, True)
            norm_root(96)
            def hidden(feeding=False, hook=None):
                if feeding:
                    feed_weights(x_hi, x_lo, norm=norm_chunk)
                else:
                    weights(hook=hook)
                skip_block()
                weights()
                for r in range(R):
                    tile_done(r)
                    dve.wait_ge(sem(f"tile_out{r}"), c.value(f"tile_out{r}"))
                    if r == 0:
                        dve.wait_ge(sem("tp_done"), c.value("tp_done"))
                    dve.tensor_tensor(nat[:, r, :], ps[:, ACC + r, :], silu_g[:, r, :], ALU.mult)\
                       .then_inc(sem(f"tile_out{r}"), 1)
                for r in range(R):
                    c.next(f"tile_out{r}")

            def product_lo(i):
                lo_part(lambda t: ff_h[:, ds(i * 4 + 2 * t, 2), :], lambda t: ff_l[:, ds(i * 4 + 2 * t, 2), :], 2)

            for f0, nf in FFN_PARTS:
                hidden(feeding=f0 == 0)
                with c.loop(dve, f"ffn_in{f0}", nf - 1) as i:
                    hidden(hook=lambda j: product_lo(i) if j == 0 else None)
                product_lo(nf - 1)
                alpha = ALPHA if f0 == 0 else 1.0
                stat = f0 == FFN_PARTS[-1][0]
                if nf == 4:
                    with c.loop(dve, f"ffn_out{f0}", 4) as i:
                        weights(kts=4 * nf)
                        residual(i, alpha, stat)
                else:
                    with c.loop(dve, f"ffn_out{f0}", 2) as i:
                        for b in range(2):
                            weights(kts=4 * nf)
                            residual(i * 2 + b, alpha, stat)
            norm_root(128)
            dve.wait_ge(sem("small2"), 64)
            dve.wait_ge(sem("wf_hi"), 1)
            dve.tensor_tensor(wf2[:, :, H_B2:], wf[:, :, :], wf2[:, :, 0:H_B2].bitcast(F32), ALU.subtract)\
               .then_inc(sem("wf_split"), 1)

            def head_norm(j):
                if n == 2 or j != 0:
                    return
                for r in range(R):
                    dve.wait_ge(sem(f"tile_out{r}"), c.value(f"tile_out{r}"))
                    dve.tensor_tensor(aux_b[:, :], nat[:, r, :], nat[:, r, :], ALU.mult).then_inc(sem("dve_step"), 1)
                    dve.wait_ge(sem("dve_step"), c.next("dve_step"))
                    dve.tensor_reduce(ssq[:, r * 4:(r + 1) * 4],
                                      aux_b[:, :].rearrange("p (h d) -> p h d", h=4), AX.X, ALU.add)\
                        .then_inc(sem("dve_step"), 1)
                    dve.wait_ge(sem("dve_step"), c.next("dve_step"))
                inverse_root(ssq[:, :], 2 * 4, 1.0 / HD, EPS)
                for r in range(R):
                    x = nat[:, r, :].rearrange("p (h d) -> p h d", h=4)
                    by = rstd[:, r * 4:(r + 1) * 4].unsqueeze(2).to_broadcast([P, 4, HD])
                    ins = dve.tensor_tensor(x, x, by, ALU.mult)
                ins.then_inc(sem("nat_ready"), 1)

            for n in range(3):
                if n == 0:
                    feed_weights(x_hi, x_lo, g_col, norm_chunk)
                    dve.wait_ge(sem("squares"), 8)
                    dve.tensor_reduce(mv[:, :, 0], ssq[:, :].rearrange("p (r n) -> p r n", r=R), AX.X, ALU.add)\
                       .then_inc(sem("dve_step"), 1)
                    dve.wait_ge(sem("dve_step"), c.next("dve_step"))
                    dve.tensor_scalar(rms[:, :], mv[:, :, 0], 1.0 / D, EPS, ALU.mult, ALU.add)\
                       .then_inc(sem("var"), 1)
                    dve.wait_ge(sem("root"), c.next("root"))
                    dve.reciprocal(rms[:, :], rms[:, :]).then_inc(sem("rms_ready"), 1)
                else:
                    weights()
                skip_block()

                def k_hook(j):
                    head_norm(j)
                    if j == 3:
                        heads_in(lambda t: q2_t[:, 2 * t:2 * t + 2, :],
                                 qk_g[:, 2 * n:2 * n + 1] if n < 2 else None)
                    if n == 0 and j == 2:
                        dve.wait_ge(sem("f_done"), c.next("f_done"))
                        dve.tensor_copy(f_t[:, :], ps[0:2 * H_B2, AUX, 0:S]).then_inc(sem("f_nat"), 1)
                    if n == 0 and j == 5:
                        dve.wait_ge(sem("f_done"), c.next("f_done"))
                        for part, rest in ((0, bf_v), (1, f_a)):
                            for r in range(R):
                                z = ps[:, AUX, S + r * 8 + part * H_B2:S + r * 8 + (part + 1) * H_B2]
                                more = rest[:, :] if part == 0 else rest[:, r, :]
                                dve.scalar_tensor_tensor(out=f_a[:, r, :], in0=z, scalar=rms[:, r:r + 1], in1=more,
                                                         op0=ALU.mult, op1=ALU.add).then_inc(sem("az"), 1)
                            dve.wait_ge(sem("az"), 2 * (part + 1))
                        dve.wait_ge(sem("ln_done"), c.next("ln_done"))
                        dve.scalar_tensor_tensor(out=logf[:, :, :], in0=f_a[:, :, :], scalar=0.0, in1=f_b[:, :, :],
                                                 op0=ALU.min, op1=ALU.subtract).then_inc(sem("logf_ready"), 1)
                weights(hook=k_hook)
                skip_block()

                def g_hook(j):
                    head_norm(j)
                    if j == 3:
                        heads_in(lambda t: k2_t[:, 2 * t:2 * t + 2, :],
                                 qk_g[:, 2 * n + 1:2 * n + 2] if n < 2 else None)
                weights(hook=g_hook)
                skip_block()

                def v_hook(j):
                    if n == 0:
                        h = j // 2
                        if j == 0:
                            dve.wait_ge(sem("f_done"), c.next("f_done"))
                            dve.tensor_copy(c_q[:, :, :],
                                            ps[:, AUX, 0:8].rearrange("p (r h) -> p r h", r=R))\
                                .then_inc(sem("dve_step"), 1)
                            dve.wait_ge(sem("dve_step"), c.next("dve_step"))
                        if j % 2 == 0:
                            for t in range(R):
                                ins = dve.tensor_scalar(aux_a[:, t * S:(t + 1) * S], upto[:, t, :],
                                                        logf[:, t, h:h + 1], None, ALU.mult)
                            ins.then_inc(sem("ck_in"), 1)
                        else:
                            dve.wait_ge(sem("f_done"), c.next("f_done"))
                            for t, (lo, hi) in enumerate(TILE_COLS):
                                ins = dve.scalar_tensor_tensor(
                                    out=bias4[:, h, lo:hi], in0=ps[:, AUX, 0:hi - lo],
                                    scalar=c_q[:, t, h:h + 1], in1=causal[:, lo:hi],
                                    op0=ALU.subtract, op1=ALU.subtract)
                            ins.then_inc(sem("dve_step"), 1)
                            dve.wait_ge(sem("dve_step"), c.next("dve_step"))
                    if j == 3:
                        heads_in(lambda t: s2_t[:, 2 * t:2 * t + 2, :])
                    if n == 1 and j >= 4:
                        h = j - 4
                        if h == 0:
                            dve.wait_ge(sem("rel"), 16 * 8)
                            dve.wait_ge(sem("t_done"), c.value("t_done"))
                        for lo, hi in TILE_COLS:
                            ins = dve.tensor_copy(logits[:, 0, lo:hi], bias4[:, h, lo:hi][:, ::-1])
                        ins.then_inc(sem("dve_step"), 1)
                        dve.wait_ge(sem("dve_step"), c.next("dve_step"))
                        dve.tensor_copy(bias4[:, h, :], logits[:, 0, 0:CW]).then_inc(sem("dve_step"), 1)
                        dve.wait_ge(sem("dve_step"), c.next("dve_step"))
                        for _, hi in TILE_COLS:
                            ins = dve.memset(bias4[0:CHUNK, h, hi - CHUNK:hi], NEG)
                        ins.then_inc(sem("dve_step"), 1)
                        dve.wait_ge(sem("dve_step"), c.next("dve_step"))
                weights(hook=v_hook)
                skip_block()
                c.mark(f"q2_{n}", "tp_free")
                c.mark(f"v2_{n}", "tile_out1")
                c.mark(f"branch{n}s", "s_done")
                c.per[("mark", f"branch{n}o")] = 1 + c.value("oh_done")
                dve.wait_ge(sem("vec"), 144 + 16 * n)
                if n == 2:
                    dve.wait_ge(sem("summed"), c.at("summed_b1"))
                with c.loop(dve, f"branch{n}", 4) as i:
                    def soft(j):
                        if j == 0:
                            softmax(flat(bias4[:, ds(i, 1), :]), ALU.subtract if n == 0 else ALU.add)
                        if j == 3:
                            c.next("t_done")

                    def stick(j):
                        if j == 0:
                            dve.wait_ge(sem("s_done"), c.next("s_done"))
                            dve.wait_ge(sem("t_done"), c.value("t_done"))
                            dve.tensor_scalar(logits[:, 1, 0:CW], ps[:, SC, 0:CW], SCALE, None, ALU.mult)\
                                .then_inc(sem("s_read"), 1)
                            dve.wait_ge(sem("s_read"), c.next("s_read"))
                            dve.wait_ge(sem("ln_done"), c.next("ln_done"))
                            dve.scalar_tensor_tensor(out=aux_b[:, 0:CW], in0=logits[:, 1, 0:CW], scalar=0.0,
                                                     in1=aux_b[:, 0:CW], op0=ALU.max, op1=ALU.add)\
                                .then_inc(sem("dve_step"), 1)
                            dve.wait_ge(sem("dve_step"), c.next("dve_step"))
                            dve.tensor_tensor(aux_b[:, 0:CW], aux_b[:, 0:CW], strict_t[:, :], ALU.add)\
                                .then_inc(sem("dve_step"), 1)
                            dve.wait_ge(sem("dve_step"), c.next("dve_step"))
                            dve.tensor_scalar(aux_b[:, 0:CW], aux_b[:, 0:CW], 0.0, None, ALU.max)\
                                .then_inc(sem("p_ready"), 1)
                            dve.wait_ge(sem("p_ready"), c.next("p_ready"))
                            dve.tensor_tensor(logits[:, 1, 0:CW], logits[:, 1, 0:CW], strict_t[:, :],
                                              ALU.add).then_inc(sem("dve_step"), 1)
                            dve.wait_ge(sem("dve_step"), c.next("dve_step"))
                        if j == 3:
                            dve.wait_ge(sem("t_done"), c.next("t_done"))
                            dve.tensor_tensor(logits[:, 0, 0:CW], logits[:, 1, 0:CW], ps[:, PT, 0:CW],
                                              ALU.subtract).then_inc(sem("nmax"), 1)
                            c.next("pt_ready")

                    def both(j):
                        (soft if n < 2 else stick)(j)
                        if j == 5:
                            dve.wait_ge(sem("o_done"), c.next("o_done"))
                            dve.tensor_tensor(aux_a[:, 0:S], ps[:, OT, 0:S], flat(s2_t[:, ds(i, 1), :]),
                                              ALU.mult).then_inc(sem("y_ready"), 1)
                            dve.wait_ge(sem("y_ready"), c.next("y_ready"))
                            dve.wait_ge(sem("oh_done"), c.next("oh_done"))
                            dve.tensor_tensor(flat(y_l[:, ds(i, 1), :]), aux_a[:, 0:S],
                                              flat(y_h[:, ds(i, 1), :]).bitcast(F32), ALU.subtract)\
                               .then_inc(sem("o_free"), 1)
                        if j == 7:
                            gates_in(gate2, vec_a, i, rms)
                    weights(hook=both)
                c.mark(f"gates2_{n}", "tile_out1")
                if n == 0:
                    c.mark("forget", "s_read")
                c.mark(f"ups{n}", "tile_out1")
                with c.loop(dve, f"up2_{n}", 2) as i:
                    for b in range(2):
                        weights(kts=4)
                        gated(gate2, merged2, i * 2 + b, n > 0)
            feed_weights(x_hi, x_lo)
            for b in range(4):
                if b > 0:
                    weights()
                residual(b, 1.0, False)
                c.mark(f"final{b}", "tile_out1")


_INS = {
    "x": ("x", (S, D)), "mem": ("mem", (S, D)), "w_in": ("w_in", (D, C_GB + D)), "b_gate": ("b_gate", (2, D)),
    "kv_norm_g": ("kv_norm_g", (LAT,)), "idx_k_norm_g": ("idx_k_norm_g", (IDX_D,)),
    "idx_k_norm_b": ("idx_k_norm_b", (IDX_D,)), "w_uk": ("w_uk", (H_DSA * HD, LAT)),
    "w_uv": ("w_uv", (H_DSA * LAT, HD)), "w_o_dsa": ("w_o_dsa", (H_DSA * HD, D)),
    "w_o_moba": ("w_o_moba", (H_MOBA * HD, D)), "w_out": ("w_out", (D, D)),
    "w_q_mem": ("w_q_mem", (D, H_MEM * HD)), "w_kv_mem": ("w_kv_mem", (D, 2 * H_MEM * HD)),
    "w_o_mem": ("w_o_mem", (H_MEM * HD, D)), "w_ffn_in": ("w_ffn_in", (D, 2 * D_FF)),
    "w_ffn_out": ("w_ffn_out", (D_FF, D)), "ln_g": ("ln_g", (3, D)), "ln_b": ("ln_b", (3, D)),
    "norm_g": ("norm_g_2", (D,)), "w_in_2": ("w_in_2", (D, C_G2 + 3 * D)), "b_f": ("b_f_2", (H_B2,)),
    "b_gate_2": ("b_gate_2", (1, 3 * D)), "qk_norm_g": ("qk_norm_g_2", (4, HD)),
    "rel_bias": ("rel_bias_2", (H_B2, 2 * MAX_REL + 1)), "w_up_2": ("w_up_2", (3 * BR_W, D)),
    "w_out_2": ("w_out_2", (D, D)),
}


def lay_out(nc, shapes, per):
    a = {k: nc.dram_tensor("in_" + k, list(s), F32, kind="ExternalInput").ap() for k, s in shapes.items()}
    out = nc.dram_tensor("out", [S, D], F32, kind="ExternalOutput").ap()
    two_blocks(nc, a, out, per)


def kernel(**inputs):
    import numpy as np
    import concourse.bacc as bacc
    from concourse.bass_utils import run_bass_kernel_spmd

    shapes = {k: s for k, (_, s) in _INS.items()}
    per = {"counting": 1}
    lay_out(bacc.Bacc("TRN2", target_bir_lowering=False, num_devices=1), shapes, per)
    del per["counting"]
    nc = bacc.Bacc("TRN2", target_bir_lowering=False, num_devices=1)
    lay_out(nc, shapes, per)
    arrays = {"in_" + k: np.ascontiguousarray(inputs[name]).reshape(s) for k, (name, s) in _INS.items()}
    r = run_bass_kernel_spmd(nc, [arrays], core_ids=[0])
    return r.results[0]["out"].reshape(1, S, D)
```
